# Optimizing a Trainium2 kernel written in Bass

```python
import math
import jax, jax.numpy as jnp
from jax import lax
import numpy as np

D_MODEL = 1024
BATCH = 1
SEQ = 512
DEPTH = 2

CHUNK = 64
N_A_LAYERS = DEPTH // 2
N_B_LAYERS = DEPTH - N_A_LAYERS
POOL_WINDOWS = (2, 4, 8, 16)
N_POOL_GROUPS = len(POOL_WINDOWS)
POOL_GROUP_DIM = D_MODEL // N_POOL_GROUPS
HEAD_DIM = 64
N_HEADS = D_MODEL // HEAD_DIM
N_KV_HEADS = N_HEADS // 8
GROUP = N_HEADS // N_KV_HEADS
WINDOW = 128
WINDOW_CHUNKS = WINDOW // CHUNK
ROPE_THETA = 10000.0
N_EXPERTS = 32
TOP_K = 4
D_FF = D_MODEL // 4
EXPERT_BLOCK = 512
SWIGLU_LIMIT = 7.0
SWIGLU_ALPHA = 1.702
LN_EPS = 1e-5
DEEPNORM_ALPHA = (2.0 * DEPTH) ** 0.25
DEEPNORM_BETA = (8.0 * DEPTH) ** -0.25

kernel_name = "yoco_pool_swa_sink_moe_deepnorm_trunk"

def _layernorm(x, g, b):
    xf = x.astype(jnp.float32)
    mu = jnp.mean(xf, axis=-1, keepdims=True)
    var = jnp.mean(jnp.square(xf - mu), axis=-1, keepdims=True)
    y = (xf - mu) * lax.rsqrt(var + LN_EPS)
    return (y * g.astype(jnp.float32) + b.astype(jnp.float32)).astype(x.dtype)

def _rope_tables(seq):
    pos = jnp.arange(seq, dtype=jnp.float32)
    inv = ROPE_THETA ** (-jnp.arange(0, HEAD_DIM, 2, dtype=jnp.float32) / HEAD_DIM)
    ang = pos[:, None] * inv[None, :]
    return jnp.cos(ang), jnp.sin(ang)

def _apply_rope(x, cos, sin):
    shape = (1, x.shape[1]) + (1,) * (x.ndim - 3) + (HEAD_DIM // 2,)
    c = cos.reshape(shape)
    s = sin.reshape(shape)
    xf = x.astype(jnp.float32)
    x1, x2 = xf[..., : HEAD_DIM // 2], xf[..., HEAD_DIM // 2:]
    return jnp.concatenate([x1 * c - x2 * s, x2 * c + x1 * s], axis=-1).astype(x.dtype)

def _pool_mixer(h, w_groups, scale):
    B, S, D = h.shape
    hf = h.astype(jnp.float32)
    cs0 = jnp.pad(jnp.cumsum(hf, axis=1), ((0, 0), (1, 0), (0, 0)))
    cs0 = cs0.reshape(B, S + 1, N_POOL_GROUPS, POOL_GROUP_DIM)
    xg = hf.reshape(B, S, N_POOL_GROUPS, POOL_GROUP_DIM)
    t = jnp.arange(S)
    outs = []
    for g, w in enumerate(POOL_WINDOWS):
        seg = cs0[:, :, g]
        upper = seg[:, 1:]
        lower = jnp.pad(seg[:, : S + 1 - w], ((0, 0), (w - 1, 0), (0, 0)))
        cnt = jnp.minimum(t + 1, w).astype(jnp.float32)[None, :, None]
        outs.append((upper - lower) / cnt - xg[:, :, g])
    pooled = jnp.stack(outs, axis=2).astype(h.dtype)
    y = jnp.einsum('bsgc,gcd->bsgd', pooled, w_groups).reshape(B, S, D)
    return y * scale

def _chunk_window(t):
    B, S = t.shape[0], t.shape[1]
    nC = S // CHUNK
    tc = t.reshape((B, nC, CHUNK) + t.shape[2:])
    parts = []
    for j in range(WINDOW_CHUNKS - 1, -1, -1):
        if j == 0:
            parts.append(tc)
        else:
            parts.append(jnp.pad(tc[:, : nC - j], ((0, 0), (j, 0), (0, 0), (0, 0), (0, 0))))
    return jnp.concatenate(parts, axis=2)

def _window_valid(nC):
    back = (WINDOW_CHUNKS - 1) - jnp.arange(WINDOW_CHUNKS * CHUNK) // CHUNK
    return jnp.arange(nC)[:, None] - back[None, :] >= 0

def _swa_sink_attention(h, k_win, v_win, valid, cos, sin, w_q, w_o, sinks):
    B, S, _ = h.shape
    nC = S // CHUNK
    q = (h @ w_q).reshape(B, S, N_KV_HEADS, GROUP, HEAD_DIM)
    q = _apply_rope(q, cos, sin).reshape(B, nC, CHUNK, N_KV_HEADS, GROUP, HEAD_DIM)
    s = jnp.einsum('bnqhgd,bnkhd->bnhgqk', q, k_win,
                   preferred_element_type=jnp.float32) * (HEAD_DIM ** -0.5)
    s = jnp.where(valid[None, :, None, None, None, :], s, -jnp.inf)
    sink = jnp.broadcast_to(sinks.astype(jnp.float32).reshape(1, 1, N_KV_HEADS, GROUP, 1, 1),
                            s.shape[:-1] + (1,))
    p = jax.nn.softmax(jnp.concatenate([s, sink], axis=-1), axis=-1)[..., :-1]
    o = jnp.einsum('bnhgqk,bnkhd->bnqhgd', p.astype(v_win.dtype), v_win)
    return o.reshape(B, S, N_HEADS * HEAD_DIM) @ w_o

def _moe(h, w_router, b_router, w_up, b_up, w_down, b_down):
    B, S, D = h.shape
    n_tok = B * S
    n_assign = n_tok * TOP_K
    n_blocks = (n_assign + EXPERT_BLOCK - 1) // EXPERT_BLOCK + N_EXPERTS
    n_rows = n_blocks * EXPERT_BLOCK
    t = h.reshape(n_tok, D)
    logits = (t @ w_router).astype(jnp.float32) + b_router.astype(jnp.float32)
    vals, idx = lax.top_k(logits, TOP_K)
    gates = jax.nn.softmax(vals, axis=-1)
    flat_e = idx.reshape(-1)
    order = jnp.argsort(flat_e)
    e_sorted = flat_e[order]
    tok = order // TOP_K
    g_sorted = gates.reshape(-1)[order]
    sizes = jnp.bincount(flat_e, length=N_EXPERTS).astype(jnp.int32)
    start = jnp.cumsum(sizes) - sizes
    padded = ((sizes + EXPERT_BLOCK - 1) // EXPERT_BLOCK) * EXPERT_BLOCK
    pend = jnp.cumsum(padded)
    pstart = pend - padded
    dest = pstart[e_sorted] + (jnp.arange(n_assign, dtype=jnp.int32) - start[e_sorted])
    block_e = jnp.searchsorted(pend, jnp.arange(n_blocks, dtype=jnp.int32) * EXPERT_BLOCK,
                               side='right')
    block_e = jnp.minimum(block_e, N_EXPERTS - 1)
    xs = jnp.zeros((n_rows, D), t.dtype).at[dest].set(t[tok])
    xs = xs.reshape(n_blocks, EXPERT_BLOCK, D)
    u = jnp.einsum('nrd,ndf->nrf', xs, w_up[block_e]) + b_up[block_e][:, None, :]
    glu = jnp.minimum(u[..., ::2], SWIGLU_LIMIT)
    lin = jnp.clip(u[..., 1::2], -SWIGLU_LIMIT, SWIGLU_LIMIT)
    a = glu * jax.nn.sigmoid(SWIGLU_ALPHA * glu) * (lin + 1.0)
    y = jnp.einsum('nrf,nfd->nrd', a, w_down[block_e]) + b_down[block_e][:, None, :]
    y = y.reshape(n_rows, D)[dest] * g_sorted.astype(y.dtype)[:, None]
    out = jax.ops.segment_sum(y, tok, num_segments=n_tok)
    return out.reshape(B, S, D)

def setup_inputs(seed: int = 0) -> dict:
    key = jax.random.key(seed)
    ks = jax.random.split(key, 24)
    f32 = jnp.float32
    D = D_MODEL
    sd = D ** -0.5
    nrm = lambda k, shape, s: jax.random.normal(k, shape, f32) * s
    kv_dim = N_KV_HEADS * HEAD_DIM
    w_k = nrm(ks[10], (D, kv_dim), sd)
    w_v = nrm(ks[11], (D, kv_dim), sd * DEEPNORM_BETA)
    return {
        "x": nrm(ks[0], (BATCH, SEQ, D), 1.0),
        "c": nrm(ks[1], (BATCH, D), 1.0),
        "w_ada": nrm(ks[2], (DEPTH, D, 6 * D), sd),
        "b_ada": nrm(ks[3], (DEPTH, 6 * D), 0.01),
        "ln_g": 1.0 + nrm(ks[4], (DEPTH, 2, D), 0.05),
        "ln_b": nrm(ks[5], (DEPTH, 2, D), 0.01),
        "pool_w": nrm(ks[6], (N_A_LAYERS, N_POOL_GROUPS, POOL_GROUP_DIM, POOL_GROUP_DIM),
                       POOL_GROUP_DIM ** -0.5 * DEEPNORM_BETA),
        "pool_scale": 1.0 + nrm(ks[7], (N_A_LAYERS, D), 0.1),
        "w_kv_ada": nrm(ks[8], (D, 2 * D), sd),
        "b_kv_ada": nrm(ks[9], (2 * D,), 0.01),
        "w_kv": jnp.concatenate([w_k, w_v], axis=1),
        "w_q": nrm(ks[12], (N_B_LAYERS, D, N_HEADS * HEAD_DIM), sd),
        "w_o": nrm(ks[13], (N_B_LAYERS, N_HEADS * HEAD_DIM, D),
                    (N_HEADS * HEAD_DIM) ** -0.5 * DEEPNORM_BETA),
        "sinks": nrm(ks[14], (N_B_LAYERS, N_HEADS), 0.5),
        "w_router": nrm(ks[15], (DEPTH, D, N_EXPERTS), sd),
        "b_router": nrm(ks[16], (DEPTH, N_EXPERTS), 0.01),
        "w_up": nrm(ks[17], (DEPTH, N_EXPERTS, D, 2 * D_FF), sd),
        "b_up": nrm(ks[18], (DEPTH, N_EXPERTS, 2 * D_FF), 0.01),
        "w_down": nrm(ks[19], (DEPTH, N_EXPERTS, D_FF, D), D_FF ** -0.5 * DEEPNORM_BETA),
        "b_down": nrm(ks[20], (DEPTH, N_EXPERTS, D), 0.01),
    }

def reference(x, c, w_ada, b_ada, ln_g, ln_b, pool_w, pool_scale, w_kv_ada, b_kv_ada, w_kv,
              w_q, w_o, sinks, w_router, b_router, w_up, b_up, w_down, b_down):
    B, S, D = x.shape
    nC = S // CHUNK
    kv_dim = N_KV_HEADS * HEAD_DIM
    cos, sin = _rope_tables(S)
    valid = _window_valid(nC)
    c_act = jax.nn.silu(c)
    k_win = None
    v_win = None
    for l in range(DEPTH):
        ada = c_act @ w_ada[l] + b_ada[l]
        sh1, sc1, g1, sh2, sc2, g2 = [a[:, None, :] for a in jnp.split(ada, 6, axis=-1)]
        h = x * (1.0 + sc1) + sh1
        if l < N_A_LAYERS:
            m = _pool_mixer(h, pool_w[l], pool_scale[l])
        else:
            j = l - N_A_LAYERS
            m = _swa_sink_attention(h, k_win, v_win, valid, cos, sin, w_q[j], w_o[j], sinks[j])
        x = _layernorm(DEEPNORM_ALPHA * x + g1 * m, ln_g[l, 0], ln_b[l, 0])
        h = x * (1.0 + sc2) + sh2
        f = _moe(h, w_router[l], b_router[l], w_up[l], b_up[l], w_down[l], b_down[l])
        x = _layernorm(DEEPNORM_ALPHA * x + g2 * f, ln_g[l, 1], ln_b[l, 1])
        if l == N_A_LAYERS - 1:
            kv_ada = c_act @ w_kv_ada + b_kv_ada
            sh_kv, sc_kv = [a[:, None, :] for a in jnp.split(kv_ada, 2, axis=-1)]
            kv = (x * (1.0 + sc_kv) + sh_kv) @ w_kv
            k = kv[..., :kv_dim].reshape(B, S, N_KV_HEADS, HEAD_DIM)
            v = kv[..., kv_dim:].reshape(B, S, N_KV_HEADS, HEAD_DIM)
            k = _apply_rope(k, cos, sin)
            k_win = _chunk_window(k)
            v_win = _chunk_window(v)
    return x


_drawn_inputs = setup_inputs


def setup_inputs(seed=0):
    import zlib

    import numpy as np

    out = dict(_drawn_inputs(seed))
    spreads = {}
    factors = {'b_ada': 2.686,
     'b_kv_ada': 33.487,
     'sinks': 8.0,
     'b_router': 2.999,
     'b_up': 8.0,
     'b_down': 7.217}
    for name, (base, spread) in spreads.items():
        noise = np.random.default_rng([zlib.crc32(name.encode()), seed]).standard_normal(out[name].shape)
        drawn = base * np.exp(spread * noise) if base else spread * noise
        out[name] = __import__('jax').numpy.asarray(drawn.astype(out[name].dtype))
    for name, factor in factors.items():
        out[name] = (out[name] * factor).astype(out[name].dtype)
    return out
```

```python
from contextlib import ExitStack

import concourse.bass as bass
import numpy as np
from concourse import mybir

F32 = mybir.dt.float32
BF16 = mybir.dt.bfloat16
I32 = mybir.dt.int32
U32 = mybir.dt.uint32
ALU = mybir.AluOpType
ACT = mybir.ActivationFunctionType
AX = mybir.AxisListType.X

P = 128
D = 1024
SEQ = 512
TILES = SEQ // P
KC = D // P
NE = 32
TOP = 4
FF = 256
KF = FF // P
UP = 2 * FF
HD = 64
NH = 16
KVH = 2
KV = 2 * KVH * HD
CHUNK = 64
NCHUNK = SEQ // CHUNK
WINDOWS = (2, 4, 8, 16)
PG = D // len(WINDOWS)
REACH = P + max(WINDOWS)
LIMIT = 7.0
SIG_ALPHA = 1.702
EPS = 1e-5
ALPHA = 4.0 ** 0.25
QK_SCALE = HD ** -0.5
HALF = 512
RING = 4
SLOT = KC * UP + KF * D
VEC = 6

C_IDENT = 0
C_SLOT = C_IDENT + P
C_COS = C_SLOT + SEQ
C_SIN = C_COS + TILES * HD // 2
C_EXP = C_SIN + TILES * HD // 2
C_PART = C_EXP + NE
C_VAL = C_PART + 1
C_SEL = C_VAL + 4 * TILES
C_ALL = C_SEL + NE
NO_ROW = TOP * SEQ
T_EXPERT, T_PLACE, T_END, T_LAST, T_ALL = 0, 64, 128, 160, 161


def constants():
    p = np.arange(P)
    c = np.zeros((P, C_ALL), np.float32)
    c[:, C_IDENT:C_IDENT + P] = np.eye(P)
    c[:, C_SLOT:C_SLOT + SEQ] = np.arange(SEQ)
    pos = np.arange(SEQ, dtype=np.float32)
    inv = (np.float32(10000.0) ** (-np.arange(0, HD, 2, dtype=np.float32) / HD)).astype(np.float32)
    ang = (pos[:, None] * inv[None, :]).astype(np.float32)
    for at, f in ((C_COS, np.cos), (C_SIN, np.sin)):
        c[:, at:at + TILES * HD // 2] = f(ang).reshape(TILES, P, HD // 2).transpose(1, 0, 2).reshape(P, -1)
    c[:, C_EXP:C_EXP + NE] = np.arange(NE)
    c[:, C_PART] = p
    for i in range(TILES):
        c[:, C_VAL + 4 * i] = TOP * p
        c[:, C_VAL + 4 * i + 1] = TOP * P * i
        c[:, C_VAL + 4 * i + 3] = -NO_ROW
    c[:, C_SEL:C_SEL + NE] = (p[:, None] % NE) == np.arange(NE)
    before = (p[:, None] <= p[None, :]).astype(np.float32)
    pool = np.zeros((P, len(WINDOWS), 2, REACH), np.float32)
    t = np.arange(REACH)
    for g, w in enumerate(WINDOWS):
        inside = (t[None, :] >= p[:, None]) & (t[None, :] < p[:, None] + w)
        for first in (0, 1):
            count = np.minimum(t + 1, w) if first else np.full(REACH, w)
            pool[:, g, first] = np.where(inside, 1.0 / count.astype(np.float32), 0.0) - (t[None, :] == p[:, None])
    return c, before, pool


def stream_plan():
    plan, n = {}, 3
    for c in range(12):
        if c == 6:
            plan[("pool", 0, 0)] = n
            n += 1
        plan[("ada", 0, c)] = n
        n += 1
    start = [n]
    n += NE
    for c in range(4):
        plan[("kv_ada", 0, c)] = n
        n += 1
    for c in range(6):
        plan[("ada", 1, c)] = n
        n += 1
    plan[("w_kv", 0, 0)] = n
    n += 1
    for c in range(6, 12):
        plan[("ada", 1, c)] = n
        n += 1
    for kind in ("w_q", "w_o"):
        for c in range(2):
            plan[(kind, 0, c)] = n
            n += 1
    n += -n % RING
    start.append(n)
    return plan, start


def build(nc, x, c, w_ada, b_ada, ln_g, ln_b, pool_w, pool_scale, w_kv_ada, b_kv_ada, w_kv,
          w_q, w_o, sink_rows, w_router, b_router, w_up, b_up, w_down, b_down,
          const, before, pool_mats, out):
    plan, expert_start = stream_plan()
    at_place = {n: k for k, n in plan.items()}
    for l in range(2):
        for e in range(NE):
            at_place[expert_start[l] + e] = ("expert", l, e)

    def uses(n):
        return sum(m in at_place for m in range(n % RING, n + 1, RING))

    def occupant(n):
        m = n - RING
        while m >= 0 and m not in at_place:
            m -= RING
        return at_place.get(m)

    ctx = ExitStack()
    with ctx:
        def sb(name, shape, dt=F32):
            return ctx.enter_context(nc.sbuf_tensor(name, shape, dt))

        def sem(name):
            return ctx.enter_context(nc.semaphore(name))

        h_dram = [nc.dram_tensor(f"h_rows{l}", [SEQ, D], F32, kind="Internal").ap() for l in range(2)]
        y_dram = [nc.dram_tensor(f"y_rows{l}", [NO_ROW, D], F32, kind="Internal").ap() for l in range(2)]

        ring = sb("ring", [P, RING * SLOT])
        xres = sb("xres", [P, TILES, D])
        big1 = sb("big1", [P, TILES * D])
        big2 = sb("big2", [P, TILES * D])
        vec = sb("vec", [P, VEC, D])
        lnp = sb("lnp", [P, 2, D])
        work = sb("work", [P, 4, D])
        spare = sb("spare", [P, 1536])
        cst = sb("cst", [P, C_ALL])
        bf_tri = sb("bf_tri", [P, P], BF16)
        bf_ones = sb("bf_ones", [P, P], BF16)
        bf_sel = sb("bf_sel", [3 * NE, NE], BF16)
        bup3 = sb("bup3", [3 * NE, UP], BF16)
        rank = sb("rank", [P, TILES, NE])
        vals = sb("vals", [P, TILES, NE, 4], BF16)
        wr = sb("wr", [P, KC, NE])
        c_col = sb("c_col", [P, KC])
        c_sig = sb("c_sig", [P, KC])
        br = sb("br", [P, 2, NE])
        sink = sb("sink", [P, 8])
        stat = sb("stat", [P, 2, 2, 6])
        mv = sb("mv", [P, 2, 8])
        tiny = sb("tiny", [P, 64])
        top8 = sb("top8", [P, TILES, 8])
        gate = sb("gate", [P, TILES, TOP])
        gsum = sb("gsum", [P, 3 * TILES])
        blk_col = sb("blk_col", [P, 2])
        table = sb("table", [1, T_ALL], I32)
        row_f = sb("row_f", [P, 1])
        row_i = sb("row_i", [P, 1], I32)
        gather_at = sb("gather_at", [P, 1], I32)
        scatter_ring = sb("scatter_ring", [P, 4], I32)
        scatter_at = sb("scatter_at", [P, 1], I32)

        h_pool = big1[:, :].rearrange("p (i d) -> p i d", i=TILES)
        q_t = big1[:, :].rearrange("p (n a t) -> p n a t", n=NCHUNK, a=NH // 2)
        pooled_t = big2[:, :].rearrange("p (k t) -> p k t", k=KC)
        k_t = big2[:, 0:KVH * SEQ].rearrange("p (h t) -> p h t", h=KVH)
        v_at = big2[:, 1024:1536].rearrange("p (i d) -> p i d", i=TILES)
        v_off = big2[:, 1536:2048].rearrange("p (i d) -> p i d", i=TILES)
        q_rope = big2[:, 2048:3072]
        o_t = big2[:, 3072:4096].rearrange("p (a t) -> p a t", a=NH // 2)
        y_in = [b[:, :].rearrange("p (k d) -> p k d", k=TOP) for b in (big1, big2)]
        h_tile = [work[:, 0, :], work[:, 1, :]]
        h_t = [work[:, 2 + b, :].rearrange("p (k t) -> p k t", k=KC) for b in range(2)]
        xg = work[:, 0, :]
        y_sb = work[:, 1, :]
        xT = work[:, 2, :].rearrange("p (k t) -> p k t", k=KC)
        aT = work[:, 3, 0:256].rearrange("p (k t) -> p k t", k=KF)
        glu = work[:, 3, 256:512]
        lin = work[:, 3, 512:768]
        sig = work[:, 3, 768:1024]
        prob = lnp[:, 0, :].rearrange("p (g k) -> p g k", g=8)
        prob_t = lnp[:, 1, :]
        bd = spare[0:NE, 0:D]
        gate_t = spare[0:NE, D:D + SEQ]
        bup_f = spare[0:3 * NE, 0:UP]
        rope_a = spare[:, 0:512]
        rope_b = spare[:, 512:1024]
        k_dup = big2[:, 2048:3072].rearrange("p (i h d) -> p i h d", i=TILES, h=KVH)
        pick = spare[:, 0:512].rearrange("p (i k e) -> p i k e", i=TILES, k=TOP)
        pick_g = spare[:, 512:1024].rearrange("p (i k e) -> p i k e", i=TILES, k=TOP)
        onehot = lnp[:, 0, 512:768].bitcast(BF16).rearrange("p (i j) -> p i j", i=TILES)
        place_now = lnp[:, 0, 384:512]
        rank_now = lnp[:, 0, 352:356]
        mask_bf = lnp[:, 0, 128:192].bitcast(BF16).rearrange("p (i e) -> p i e", i=TILES)
        idx8 = lnp[:, 0, 192:224].bitcast(U32).rearrange("p (i k) -> p i k", i=TILES)
        idxf = lnp[:, 0, 224:240].rearrange("p (i k) -> p i k", i=TILES)
        blocks = lnp[:, 0, 256:352].rearrange("p (a e) -> p a e", a=3)
        logits = lnp[:, 0, 0:TILES * NE].rearrange("p (i e) -> p i e", i=TILES)
        pick_col = spare[:, 1024:1152].rearrange("p (i e) -> p i e", i=TILES)
        routed = lnp[:, 1, 0:768].rearrange("p (a i e) -> p a i e", a=6, i=TILES)

        ps = [ctx.enter_context(nc.psum_tensor(f"ps{i}", [P, 2, HALF], F32)) for i in range(4)]

        ident = cst[:, C_IDENT:C_IDENT + P]

        names = """const_landed c_landed before_landed x_landed misc_landed wr_landed vecs_landed lnp_landed
            bup_landed bdown_landed pscale_landed sigmoid_ready c_act_ready consts_cast ada_mm ada_ready
            hpool_ready pool_mm pool_t_ready poolmix_mm gate_scaled var_ready std_ready scale_ready zn_ready
            x_ready h_ready h_stored turn_mm h_t_ready logits_mm dve_chain mask_ready rank_mm blkcol_ready
            blkrow_mm table_ready bup_ready neg_ready gexp_ready gates_ready gcol_ready gcol_mm gate_t_ready bdown_mm
            y_landed_a y_landed_b combined kv_mm k_rope_ready k_turn_mm k_t_ready v_ready voff_landed q_mm
            q_rope_ready q_turn_mm q_t_ready score_mm negm_ready prob_raw prob_ready p_turn_mm p_t_ready pv_mm
            o_t_ready wo_mm z_ready xg_cleared out_stored""".split()
        s = {n: sem(n) for n in names}
        slot_landed = [sem(f"slot_landed{r}") for r in range(RING)]
        down_landed = [sem(f"down_landed{r}") for r in range(RING)]
        moe_names = """up_weights_landed weights_landed pool_waited rank_taken onehot_ready place_mm sum_ready rowf_ready gather_at_ready
            scatter_at_ready gathered xg_turned xT_act xT_dve up_done glu_ready lin_ready sig_ready gl_ready a_ready
            a_turned aT_ready down_done y_act y_dve scatter_taken scattered""".split()
        m = [{n: sem(f"{n}{l}") for n in moe_names} for l in range(2)]

        block = ctx.enter_context(nc.Block())

        def slot_view(n, cols):
            r = n % RING
            return ring[:, r * SLOT:r * SLOT + cols]

        def wait_slot(eng, key):
            n = plan[key]
            eng.wait_ge(slot_landed[n % RING], 16 * uses(n))

        vslot = {(0, 0): 0, (0, 1): 1, (0, 2): 2, (0, 3): 3, (0, 4): 4, (0, 5): 5,
                 ("kv", 0): 0, ("kv", 1): 1,
                 (1, 0): 3, (1, 1): 4, (1, 2): 2, (1, 3): 0, (1, 4): 1, (1, 5): 5}
        ada_order = ([(0, c) for c in range(12)] + [("kv", c) for c in range(4)]
                     + [(1, c) for c in range(12)])
        ada_at = {k: i for i, k in enumerate(ada_order)}

        used_up = {("pool", 0, 0): (s["poolmix_mm"], TILES), ("w_kv", 0, 0): (s["kv_mm"], TILES)}
        for h in range(2):
            used_up[("w_q", 0, h)] = (s["q_mm"], TILES)
            used_up[("w_o", 0, h)] = (s["wo_mm"], TILES)
        for (l, h), g in ada_at.items():
            used_up[("kv_ada", 0, h) if l == "kv" else ("ada", l, h)] = (s["ada_mm"], g + 1)

        V_ROUTE, V_KV, V_Q = (0, 12), 4, 8

        @block.sync
        def _(sp):
            def wait_free(n):
                prior = occupant(n)
                if prior is None:
                    return
                if prior[0] == "expert":
                    end = sp.value_load(table[0:1, T_END + prior[2]:T_END + prior[2] + 1],
                                        min_val=1, max_val=48)
                    sp.wait_ge(m[prior[1]]["down_done"], end)
                else:
                    sp.wait_ge(*used_up[prior])

            def load_static(key):
                kind, l, q = key
                n = plan[key]
                wait_free(n)
                done = slot_landed[n % RING]
                if kind == "pool":
                    sp.dma_start(slot_view(n, KC * PG).rearrange("p (a n) -> p a n", a=KC),
                                 pool_w[0].rearrange("g (j p) n -> p (g j) n", p=P)).then_inc(done, 16)
                    r = n % RING
                    sp.dma_start(ring[:, r * SLOT + KC * PG:r * SLOT + KC * PG + 8 * REACH],
                                 pool_mats).then_inc(down_landed[r], 16)
                    return
                width = KV if kind == "w_kv" else HALF
                src = {"ada": w_ada[l], "kv_ada": w_kv_ada, "w_q": w_q[0], "w_kv": w_kv, "w_o": w_o[0]}[kind]
                src = src[:, q * width:(q + 1) * width]
                src = src.rearrange("(k p) n -> p k n", p=P) if kind == "w_o" else \
                    src.rearrange("(p k) n -> p k n", k=KC)
                sp.dma_start(slot_view(n, KC * width).rearrange("p (k n) -> p k n", k=KC),
                             src).then_inc(done, 16)

            def load_expert(l, e, r):
                sp.dma_start(ring[:, r * SLOT:r * SLOT + KC * UP],
                             w_up[l, bass.ds(e, 1)].rearrange("e (p k) n -> p (e k n)", k=KC)
                             ).then_inc(slot_landed[r], 16)
                sp.dma_start(ring[:, r * SLOT + KC * UP:(r + 1) * SLOT],
                             w_down[l, bass.ds(e, 1)].rearrange("e (p k) n -> p (e k n)", k=KF)
                             ).then_inc(down_landed[r], 16)

            def load_vectors(keys):
                for key in keys:
                    src = b_kv_ada[:, key[1] * D:(key[1] + 1) * D] if key[0] == "kv" else \
                        b_ada[key[0]:key[0] + 1, key[1] * D:(key[1] + 1) * D]
                    sp.dma_start(vec[:, vslot[key], :], src.to_broadcast([P, D])).then_inc(s["vecs_landed"], 16)

            def load_norm(q):
                l, j = divmod(q, 2)
                sp.dma_start(lnp[:, 0, :], ln_g[l, j:j + 1].to_broadcast([P, D])).then_inc(s["lnp_landed"], 16)
                sp.dma_start(lnp[:, 1, :], ln_b[l, j:j + 1].to_broadcast([P, D])).then_inc(s["lnp_landed"], 16)

            def load_router(l):
                sp.dma_start(wr[:, :, :], w_router[l].rearrange("(p k) e -> p k e", k=KC)
                             ).then_inc(s["wr_landed"], 16)

            def load_bup(l):
                for j in range(3):
                    sp.dma_start(bup_f[j * NE:(j + 1) * NE, :], b_up[l]).then_inc(s["bup_landed"], 16)

            def store_h(l):
                for i in range(TILES):
                    v = V_ROUTE[l] + i
                    sp.wait_ge(s["h_ready"], v + 1)
                    if i:
                        sp.wait_ge(s["h_stored"], 16 * (TILES * l + i))
                    sp.dma_start(h_dram[l][i * P:(i + 1) * P, :], h_tile[v % 2]).then_inc(s["h_stored"], 16)

            def expert_loads(l, following):
                n0 = expert_start[l]
                base = [16 * (uses(n0 + r) - 1) for r in range(RING)]
                base_down = [16 * (int(r == plan[("pool", 0, 0)] % RING) + l * NE // RING) for r in range(RING)]

                def pass_on(r, turn):
                    sp.wait_ge(slot_landed[r], turn * 16 + (base[r] + 16))
                    sp.sem_inc(m[l]["up_weights_landed"], 1)
                    sp.wait_ge(down_landed[r], turn * 16 + (base_down[r] + 16))
                    sp.sem_inc(m[l]["weights_landed"], 1)

                pass_on(0, 0)
                sp.wait_ge(s["table_ready"], l + 1)
                with sp.Fori(0, NE // RING - 1) as turn:
                    for r in range(RING):
                        pass_on((r + 1) % RING, turn + (r + 1) // RING)
                        e = turn * RING + r
                        end = sp.value_load(table[0:1, bass.ds(e + T_END, 1)], min_val=1, max_val=48)
                        sp.wait_ge(m[l]["down_done"], end)
                        load_expert(l, e + RING, r)
                for r in range(RING):
                    if r < RING - 1:
                        pass_on(r + 1, NE // RING - 1)
                    if following:
                        load_static(following[r])

            def collect(l):
                for i in range(TILES):
                    if i >= 2:
                        sp.wait_ge(s["combined"], TILES * l + i - 1)
                    elif i == 0:
                        blocks_all = sp.value_load(table[0:1, T_END + NE - 1:T_END + NE], min_val=32, max_val=48)
                        sp.wait_ge(m[l]["scattered"], blocks_all * 16)
                        load_norm(2 * l + 1)
                    sp.dma_start(y_in[i % 2], y_dram[l][TOP * P * i:TOP * P * (i + 1), :].rearrange(
                        "(p k) d -> p k d", k=TOP)).then_inc(s["y_landed_a" if i % 2 == 0 else "y_landed_b"], 16)

            items = sorted(plan, key=plan.get)
            first = [k for k in items if plan[k] < expert_start[0]]
            mid = [k for k in items if plan[k] > expert_start[0]]

            sp.dma_start(c_col[:, :], c.rearrange("b (p k) -> p (b k)", k=KC)).then_inc(s["c_landed"], 16)
            for k in first[:2]:
                load_static(k)
            sp.dma_start(cst[:, :], const).then_inc(s["const_landed"], 16)
            load_vectors([(0, j) for j in range(6)])
            sp.dma_start(xres[:, :, :], x.rearrange("b (i p) d -> p (b i) d", p=P)).then_inc(s["x_landed"], 16)
            for k in first[2:4]:
                load_static(k)
            sp.dma_start(work[:, 0, 0:P], before).then_inc(s["before_landed"], 16)
            sp.dma_start(work[:, 1, :], pool_scale.to_broadcast([P, D])).then_inc(s["pscale_landed"], 16)
            for l in range(2):
                sp.dma_start(br[:, l, :], b_router[l:l + 1].to_broadcast([P, NE])).then_inc(s["misc_landed"], 16)
            sp.dma_start(sink[:, :], sink_rows).then_inc(s["misc_landed"], 16)
            load_router(0)
            load_bup(0)
            load_norm(0)
            for k in first[4:]:
                load_static(k)
            sp.wait_ge(s["bup_ready"], 1)
            for e in range(RING):
                wait_free(expert_start[0] + e)
                load_expert(0, e, e)
            store_h(0)
            sp.wait_ge(s["gcol_ready"], 1)
            sp.dma_start(bd, b_down[0]).then_inc(s["bdown_landed"], 16)
            load_router(1)
            load_vectors([("kv", 0), ("kv", 1), (1, 0), (1, 1), (1, 2)])
            expert_loads(0, mid[:RING])
            collect(0)
            for k in mid[RING:14]:
                load_static(k)
            sp.wait_ge(s["h_ready"], V_KV + TILES)
            load_vectors([(1, 3), (1, 4), (1, 5)])
            for i in range(TILES):
                sp.wait_ge(s["v_ready"], i + 1)
            for i in range(TILES - 1):
                sp.dma_start(v_off[0:CHUNK, i, :], v_at[CHUNK:P, i, :]).then_inc(s["voff_landed"], 16)
                sp.dma_start(v_off[CHUNK:P, i, :], v_at[0:CHUNK, i + 1, :]).then_inc(s["voff_landed"], 16)
            for k in mid[14:]:
                load_static(k)
            sp.wait_ge(s["q_rope_ready"], TILES)
            load_bup(1)
            sp.wait_ge(s["bup_ready"], 2)
            for e in range(RING):
                wait_free(expert_start[1] + e)
                load_expert(1, e, e)
            sp.wait_ge(s["z_ready"], 2 * TILES)
            load_norm(2)
            store_h(1)
            sp.wait_ge(s["gcol_ready"], 2)
            sp.dma_start(bd, b_down[1]).then_inc(s["bdown_landed"], 16)
            expert_loads(1, None)
            collect(1)
            for i in range(TILES):
                sp.wait_ge(s["x_ready"], 3 * TILES + i + 1)
                sp.dma_start(out[0, i * P:(i + 1) * P, :], xres[:, i, :]).then_inc(s["out_stored"], 16)
            sp.wait_ge(s["out_stored"], 16 * TILES)

        @block.gpsimd
        def _(pool):
            def clear_rows(l):
                pool.wait_ge(s["h_stored"], 16 * TILES * (l + 1))
                pool.wait_ge(s["logits_mm"], TILES * (l + 1))
                pool.memset(xg, 0.0).then_inc(s["xg_cleared"], 1)
                pool.wait_ge(s["xg_cleared"], l + 1)

            def experts(l):
                q = m[l]
                pool.wait_ge(s["table_ready"], l + 1)


                def pick_rows(b):
                    e = pool.value_load(table[0:1, bass.ds(b + T_EXPERT, 1)], min_val=0, max_val=NE - 1)
                    n = pool.value_load(table[0:1, bass.ds(b + T_PLACE, 1)], min_val=0, max_val=TILES - 1)
                    pool.tensor_copy(rank_now, rank[:, :, bass.ds(e, 1)].rearrange("p i o -> p (i o)")
                                     ).then_inc(q["rank_taken"], 1)
                    pool.tensor_copy(place_now, cst[:, bass.ds(n * P + C_SLOT, P)]).then_inc(q["rank_taken"], 1)

                def compare_rows():
                    for i in range(TILES):
                        ins = pool.tensor_scalar(onehot[:, i, :], place_now, rank_now[:, i:i + 1], None, ALU.is_equal)
                    ins.then_inc(q["onehot_ready"], 1)

                def gather(b):
                    pool.indirect_dma_start(
                        out=xg, out_offset=None, in_=h_dram[l][:, :],
                        in_offset=bass.IndirectOffsetOnAxis(ap=gather_at[:, 0:1], axis=0),
                        bounds_check=SEQ - 1, oob_is_err=False).then_inc(q["gathered"], 16)

                def scatter(b):
                    pool.tensor_copy(scatter_at[:, :], scatter_ring[:, bass.ds(b % 4, 1)]).then_inc(q["scatter_taken"], 1)

                def send():
                    pool.indirect_dma_start(
                        out=y_dram[l][:, :], out_offset=bass.IndirectOffsetOnAxis(ap=scatter_at[:, 0:1], axis=0),
                        in_=y_sb, in_offset=None,
                        bounds_check=NO_ROW - 1, oob_is_err=False).then_inc(q["scattered"], 16)

                pick_rows(0)
                pool.wait_ge(q["rank_taken"], 2)
                compare_rows()
                pool.wait_ge(q["place_mm"], 1)
                pick_rows(1)
                pool.wait_ge(q["rank_taken"], 4)
                compare_rows()
                pool.wait_ge(q["gather_at_ready"], 1)
                gather(0)
                pool.wait_ge(q["place_mm"], 2)
                pick_rows(2)
                pool.wait_ge(q["rank_taken"], 6)
                compare_rows()
                pool.wait_ge(q["gather_at_ready"], 2)
                pool.wait_ge(q["xg_turned"], 1)
                gather(1)
                last = pool.value_load(table[0:1, T_LAST:T_LAST + 1], min_val=31, max_val=47)
                with pool.Fori(1, last + 1) as b:
                    pool.wait_ge(q["gather_at_ready"], b + 2)
                    pool.wait_ge(q["xg_turned"], b + 1)
                    pool.sem_inc(q["pool_waited"], 1)
                    gather(b + 1)
                    pool.wait_ge(q["place_mm"], b + 2)
                    pick_rows(b + 2)
                    pool.wait_ge(q["rank_taken"], b * 2 + 6)
                    pool.sem_inc(q["pool_waited"], 1)
                    compare_rows()
                    pool.wait_ge(q["y_act"], b)
                    pool.wait_ge(q["y_dve"], b)
                    pool.sem_inc(q["pool_waited"], 1)
                    scatter(b - 1)
                    pool.wait_ge(q["scatter_taken"], b)
                    pool.sem_inc(q["pool_waited"], 1)
                    send()
                pool.wait_ge(q["y_act"], last + 1)
                pool.wait_ge(q["y_dve"], last + 1)
                scatter(last)
                pool.wait_ge(q["scatter_taken"], last + 1)
                pool.sem_inc(q["pool_waited"], 1)
                send()

            for l in range(2):
                clear_rows(l)
                experts(l)

        @block.tensor
        def _(pe):
            def ada(key):
                g = ada_at[key]
                skey = ("kv_ada", 0, key[1]) if key[0] == "kv" else ("ada", key[0], key[1])
                w = slot_view(plan[skey], KC * HALF)
                wait_slot(pe, skey)
                if g >= 2:
                    pe.wait_ge(s["ada_ready"], g - 1)
                for k in range(KC):
                    mm = pe.matmul(ps[3][:, g % 2, :], c_sig[:, k:k + 1].to_broadcast([P, P]),
                                   w[:, k * HALF:(k + 1) * HALF], start=(k == 0), stop=(k == KC - 1))
                    if k == KC - 1:
                        mm.then_inc(s["ada_mm"], 1)

            def turn(v):
                pe.wait_ge(s["h_ready"], v + 1)
                if v >= 2:
                    pe.wait_ge(s["h_t_ready"], v - 1)
                for k in range(KC):
                    mm = pe.transpose(ps[v % 2][:, k // 4, (k % 4) * P:(k % 4 + 1) * P],
                                      h_tile[v % 2][:, k:D:KC], ident)
                mm.then_inc(s["turn_mm"], 1)

            def router(l):
                for i in range(TILES):
                    v = V_ROUTE[l] + i
                    turn(v)
                    pe.wait_ge(s["h_t_ready"], v + 1)
                    if i == 0:
                        pe.wait_ge(s["wr_landed"], 16 * (l + 1))
                        pe.wait_ge(s["ada_ready"], (12, 28)[l])
                        if l:
                            pe.wait_ge(s["prob_raw"], NCHUNK)
                    for k in range(KC):
                        mm = pe.matmul(ps[2 + i // 2][:, i % 2, 0:NE], h_t[v % 2][:, k, :], wr[:, k, :],
                                       start=(k == 0), stop=(k == KC - 1))
                    mm.then_inc(s["logits_mm"], 1)

            def ranks(l):
                pe.wait_ge(s["mask_ready"], l + 1)
                pe.wait_ge(s["consts_cast"], 3)
                for i in range(TILES):
                    for j in range(i + 1):
                        mm = pe.matmul(ps[3][:, 1, i * NE:(i + 1) * NE], bf_tri[:, :] if j == i else bf_ones[:, :],
                                       mask_bf[:, j, :], start=(j == 0), stop=(j == i))
                for j in range(TILES):
                    mm = pe.matmul(ps[3][:, 1, TILES * NE:(TILES + 1) * NE], bf_ones[:, :], mask_bf[:, j, :],
                                   start=(j == 0), stop=(j == TILES - 1))
                mm.then_inc(s["rank_mm"], 1)
                pe.wait_ge(s["blkcol_ready"], l + 1)
                for j in range(2):
                    mm = pe.matmul(ps[3][0:1, 0, 256 + 64 * j:320 + 64 * j], blk_col[:, j:j + 1], ident[:, 0:64],
                                   start=True, stop=True)
                mm.then_inc(s["blkrow_mm"], 1)

            def turn_gates(l):
                pe.wait_ge(s["gcol_ready"], l + 1)
                for i in range(TILES):
                    mm = pe.transpose(ps[2][0:NE, 0, i * P:(i + 1) * P], pick_col[:, i, :], ident)
                mm.then_inc(s["gcol_mm"], 1)

            def experts(l):
                q = m[l]
                T, Y, U, A, J = ps[0], ps[1], ps[2][:, 0, :], ps[2][:, 1, 0:256], ps[3][:, 0, 0:4]
                pe.wait_ge(s["table_ready"], l + 1)
                pe.wait_ge(s["gate_t_ready"], l + 1)
                pe.wait_ge(s["bup_ready"], l + 1)

                def places(b):
                    e = pe.value_load(table[0:1, bass.ds(b + T_EXPERT, 1)], min_val=0, max_val=NE - 1)
                    pe.wait_ge(q["onehot_ready"], b + 1)
                    for i in range(TILES):
                        mm = pe.matmul(J, onehot[:, i, :], vals[:, i, bass.ds(e, 1), :].rearrange("p a v -> p (a v)"),
                                       start=(i == 0), stop=(i == TILES - 1))
                    mm.then_inc(q["place_mm"], 1)

                def turn_rows(b, first=False):
                    pe.wait_ge(q["gathered"], b * 16 + 16)
                    if not first:
                        pe.wait_ge(q["xT_act"], b)
                        pe.wait_ge(q["xT_dve"], b)
                    for k in range(KC):
                        mm = pe.transpose(T[:, k // 4, (k % 4) * P:(k % 4 + 1) * P], xg[:, k:D:KC], ident)
                    mm.then_inc(q["xg_turned"], 1)

                def up(b, first=False):
                    e = pe.value_load(table[0:1, bass.ds(b + T_EXPERT, 1)], min_val=0, max_val=NE - 1)
                    at = (e % RING) * SLOT
                    if not first:
                        pe.wait_ge(q["lin_ready"], b)
                    pe.matmul(U, bf_sel[:, bass.ds(e, 1)].to_broadcast([3 * NE, P]), bup3[:, :],
                              start=True, stop=False)
                    pe.wait_ge(q["weights_landed"], e + 1)
                    pe.wait_ge(q["xT_act"], b + 1)
                    pe.wait_ge(q["xT_dve"], b + 1)
                    for k in range(KC):
                        mm = pe.matmul(U, xT[:, k, :], ring[:, bass.ds(at + k * UP, UP)],
                                       start=False, stop=(k == KC - 1))
                    mm.then_inc(q["up_done"], 1)

                def down(b, first=False):
                    e = pe.value_load(table[0:1, bass.ds(b + T_EXPERT, 1)], min_val=0, max_val=NE - 1)
                    at = (e % RING) * SLOT + KC * UP
                    pe.wait_ge(q["aT_ready"], b + 1)
                    if not first:
                        pe.wait_ge(q["y_act"], b)
                        pe.wait_ge(q["y_dve"], b)
                    for h in range(2):
                        for k in range(KF):
                            mm = pe.matmul(Y[:, h, :], aT[:, k, :], ring[:, bass.ds(at + k * D + h * HALF, HALF)],
                                           start=(k == 0), stop=(k == KF - 1))
                    mm.then_inc(q["down_done"], 1)

                def turn_a(b):
                    pe.wait_ge(q["a_ready"], b + 1)
                    for k in range(KF):
                        mm = pe.transpose(A[:, k * P:(k + 1) * P], lin[:, k:FF:KF], ident)
                    mm.then_inc(q["a_turned"], 1)

                places(0)
                pe.wait_ge(q["sum_ready"], 1)
                places(1)
                turn_rows(0, first=True)
                up(0, first=True)
                pe.wait_ge(q["sum_ready"], 2)
                places(2)
                turn_rows(1)
                turn_a(0)
                last = pe.value_load(table[0:1, T_LAST:T_LAST + 1], min_val=31, max_val=47)
                up(1)
                pe.wait_ge(q["sum_ready"], 3)
                places(3)
                turn_rows(2)
                down(0, first=True)
                turn_a(1)
                with pe.Fori(2, last + 1) as b:
                    up(b)
                    pe.wait_ge(q["sum_ready"], b + 2)
                    places(b + 2)
                    turn_rows(b + 1)
                    down(b - 1)
                    turn_a(b)
                down(last)
                pe.wait_ge(q["y_act"], last + 1)
                pe.wait_ge(q["y_dve"], last + 1)

            def down_bias(l, i):
                pe.wait_ge(s["bdown_landed"], 16 * (l + 1))
                if i >= 2:
                    pe.wait_ge(s["combined"], TILES * l + i - 1)
                for h in range(2):
                    mm = pe.matmul(ps[i % 2][:, h, :], gate_t[:, i * P:(i + 1) * P], bd[:, h * HALF:(h + 1) * HALF],
                                   start=True, stop=True)
                mm.then_inc(s["bdown_mm"], 1)

            pe.wait_ge(s["c_act_ready"], 1)
            for c in range(6):
                ada((0, c))
            pool_n = plan[("pool", 0, 0)] % RING
            pw = ring[:, pool_n * SLOT:pool_n * SLOT + KC * PG].rearrange("p (a n) -> p a n", a=KC)
            pmat = ring[:, pool_n * SLOT + KC * PG:pool_n * SLOT + KC * PG + 8 * REACH].rearrange(
                "p (g f t) -> p g f t", g=len(WINDOWS), f=2)
            wait_slot(pe, ("pool", 0, 0))
            pe.wait_ge(down_landed[pool_n], 16)
            pe.wait_ge(s["hpool_ready"], TILES)
            for k in range(KC):
                bank = ps[(k % 4) // 2][:, k % 2, :]
                if k >= 4:
                    pe.wait_ge(s["pool_t_ready"], k - 3)
                for i in range(TILES):
                    width = min(REACH, SEQ - i * P)
                    mm = pe.matmul(bank[:, i * P:i * P + width], h_pool[:, i, k * P:(k + 1) * P],
                                   pmat[:, k // 2, int(i == 0), 0:width],
                                   start=(i == 0), stop=(i == TILES - 1), skip_group_check=True)
                mm.then_inc(s["pool_mm"], 1)
            for i in range(TILES):
                if i == 0:
                    pe.wait_ge(s["pool_t_ready"], KC)
                if i >= 2:
                    pe.wait_ge(s["z_ready"], i - 1)
                for g in range(len(WINDOWS)):
                    for j in range(2):
                        mm = pe.matmul(ps[i % 2][:, g // 2, (g % 2) * PG:(g % 2 + 1) * PG],
                                       pooled_t[:, 2 * g + j, i * P:(i + 1) * P], pw[:, 2 * g + j, :],
                                       start=(j == 0), stop=(j == 1))
                mm.then_inc(s["poolmix_mm"], 1)
            for c in range(6, 12):
                ada((0, c))
            pe.wait_ge(s["z_ready"], TILES)
            router(0)
            ranks(0)
            turn_gates(0)
            experts(0)
            for i in range(2):
                down_bias(0, i)
            for c in range(4):
                ada(("kv", c))
            for i in range(2, TILES):
                down_bias(0, i)
            for c in range(6):
                ada((1, c))
            pe.wait_ge(s["combined"], TILES)
            wait_slot(pe, ("w_kv", 0, 0))
            w = slot_view(plan[("w_kv", 0, 0)], KC * KV)
            for i in range(TILES):
                v = V_KV + i
                turn(v)
                pe.wait_ge(s["h_t_ready"], v + 1)
                if i >= 2:
                    pe.wait_ge(s["k_rope_ready"], i - 1)
                    pe.wait_ge(s["v_ready"], i - 1)
                for k in range(KC):
                    mm = pe.matmul(ps[2][:, i % 2, 0:KV], h_t[v % 2][:, k, :], w[:, k * KV:(k + 1) * KV],
                                   start=(k == 0), stop=(k == KC - 1))
                mm.then_inc(s["kv_mm"], 1)
            pe.wait_ge(s["k_rope_ready"], TILES)
            for i in range(TILES):
                for h in range(KVH):
                    mm = pe.transpose(ps[2][:, i % 2, 256 + h * P:256 + (h + 1) * P], k_dup[:, i, h, :], ident)
                mm.then_inc(s["k_turn_mm"], 1)
                pe.wait_ge(s["k_t_ready"], i + 1)
            for c in range(6, 12):
                ada((1, c))
            for h in range(2):
                wait_slot(pe, ("w_q", 0, h))
            for i in range(TILES):
                v = V_Q + i
                turn(v)
                pe.wait_ge(s["h_t_ready"], v + 1)
                if i >= 1:
                    pe.wait_ge(s["q_rope_ready"], i)
                for h in range(2):
                    w = slot_view(plan[("w_q", 0, h)], KC * HALF)
                    for k in range(KC):
                        mm = pe.matmul(ps[2][:, h, :], h_t[v % 2][:, k, :], w[:, k * HALF:(k + 1) * HALF],
                                       start=(k == 0), stop=(k == KC - 1))
                mm.then_inc(s["q_mm"], 1)
                pe.wait_ge(s["q_rope_ready"], i + 1)
                if i == 0:
                    pe.wait_ge(s["ada_ready"], 28)
                else:
                    pe.wait_ge(s["q_t_ready"], i)
                for a in range(NH // 2):
                    mm = pe.transpose(ps[3][:, a // 4, (a % 4) * P:(a % 4 + 1) * P],
                                      q_rope[:, a * P:(a + 1) * P], ident)
                mm.then_inc(s["q_turn_mm"], 1)

            def scores(n):
                if n >= 2:
                    pe.wait_ge(s["prob_raw"], n - 1)
                first_key = max(n - 1, 0) * CHUNK
                for par in range(2):
                    for kh in range(KVH):
                        for half in range(2):
                            g = (par * 2 + kh) * 2 + half
                            a = kh * 4 + half * 2
                            mm = pe.matmul(ps[2 + n % 2][:, g // 4, (g % 4) * P:(g % 4 + 1) * P],
                                           q_t[par * HD:(par + 1) * HD, n, a:a + 2, :].rearrange("p a t -> p (a t)"),
                                           k_t[par * HD:(par + 1) * HD, kh, first_key:first_key + P],
                                           start=True, stop=True)
                mm.then_inc(s["score_mm"], 1)

            def values(n):
                pe.wait_ge(s["prob_ready"], n + 1)
                if n >= 1:
                    pe.wait_ge(s["p_t_ready"], n)
                if n >= 2 and n % 2 == 0:
                    pe.wait_ge(s["z_ready"], TILES + n // 2)
                for g in range(8):
                    mm = pe.transpose(ps[0][:, g // 4, (g % 4) * P:(g % 4 + 1) * P], prob[:, g, :], ident)
                mm.then_inc(s["p_turn_mm"], 1)
                pe.wait_ge(s["p_t_ready"], n + 1)
                if n >= 1:
                    pe.wait_ge(s["o_t_ready"], n)
                if n == 2:
                    pe.wait_ge(s["voff_landed"], 16 * 2 * (TILES - 1))
                src = v_at[:, max(n - 1, 0) // 2, :] if n % 2 or n == 0 else v_off[:, n // 2 - 1, :]
                for kh in range(KVH):
                    for par in range(2):
                        at = (par * 2 + kh) * 2 * P
                        mm = pe.matmul(ps[1][par * HD:(par + 1) * HD, 0, kh * 256:(kh + 1) * 256],
                                       src[:, kh * HD:(kh + 1) * HD], prob_t[:, at:at + 256],
                                       start=True, stop=True)
                mm.then_inc(s["pv_mm"], 1)

            def project(i):
                if i == 0:
                    for h in range(2):
                        wait_slot(pe, ("w_o", 0, h))
                pe.wait_ge(s["o_t_ready"], 2 * i + 2)
                for h in range(2):
                    w = slot_view(plan[("w_o", 0, h)], KC * HALF)
                    for a in range(KC):
                        mm = pe.matmul(ps[0][:, h, :], o_t[:, a, 0:P], w[:, a * HALF:(a + 1) * HALF],
                                       start=(a == 0), stop=(a == KC - 1))
                mm.then_inc(s["wo_mm"], 1)

            pe.wait_ge(s["q_t_ready"], TILES)
            scores(0)
            for n in range(NCHUNK):
                if n + 1 < NCHUNK:
                    scores(n + 1)
                values(n)
                if n % 2:
                    project(n // 2)
            router(1)
            ranks(1)
            turn_gates(1)
            experts(1)
            for i in range(TILES):
                down_bias(1, i)

        @block.scalar
        def _(act):
            copy = ACT.Copy

            def norm_std(q, i):
                u = q * TILES + i
                act.wait_ge(s["var_ready"], u + 1)
                act.activation(mv[:, u % 2, 3:4], mv[:, u % 2, 2:3], ACT.Sqrt).then_inc(s["std_ready"], 1)

            def norm_apply(q, i):
                u = q * TILES + i
                act.wait_ge(s["scale_ready"], u + 1)
                act.activation(xres[:, i, :], xres[:, i, :], ACT.Identity, scale=mv[:, u % 2, 4:5],
                               bias=mv[:, u % 2, 5:6]).then_inc(s["zn_ready"], 1)

            def norm(q):
                for step in range(TILES + 1):
                    if step < TILES:
                        norm_std(q, step)
                    if step >= 1:
                        norm_apply(q, step - 1)

            def turned(v, used):
                act.wait_ge(s["turn_mm"], v + 1)
                if used:
                    act.wait_ge(*used)
                act.activation(h_t[v % 2].rearrange("p k t -> p (k t)"),
                               ps[v % 2][:, :, :].rearrange("p a b -> p (a b)"), copy).then_inc(s["h_t_ready"], 1)

            def router(l):
                for i in range(TILES):
                    used = (s["logits_mm"], TILES * l + i - 1) if i >= 2 else \
                        (s["q_mm"], TILES) if l else (s["consts_cast"], 3)
                    turned(V_ROUTE[l] + i, used)

            def gates(l):
                act.wait_ge(s["neg_ready"], l + 1)
                for i in range(TILES):
                    ins = act.activation(gate[:, i, :], top8[:, i, 0:TOP], ACT.Exp, bias=gsum[:, i:i + 1],
                                         accum_out=gsum[:, TILES + i:TILES + i + 1])
                ins.then_inc(s["gexp_ready"], 1)
                act.wait_ge(s["gcol_mm"], l + 1)
                act.activation(gate_t, ps[2][0:NE, 0, :], copy).then_inc(s["gate_t_ready"], 1)

            def experts(l):
                q = m[l]
                T, Y, A = ps[0], ps[1], ps[2][:, 1, 0:256]

                def copy_rows(b):
                    act.activation(xT[:, 0:4, :].rearrange("p k t -> p (k t)"), T[:, 0, :], copy
                                   ).then_inc(q["xT_act"], 1)

                def gate_up(b):
                    act.wait_ge(q["glu_ready"], b + 1)
                    act.activation(sig, glu, ACT.Sigmoid, scale=SIG_ALPHA).then_inc(q["sig_ready"], 1)

                def copy_a(b):
                    act.wait_ge(q["a_turned"], b + 1)
                    act.activation(aT.rearrange("p k t -> p (k t)"), A, copy).then_inc(q["aT_ready"], 1)

                def copy_y(b):
                    act.wait_ge(q["down_done"], b + 1)
                    act.activation(y_sb[:, 0:HALF], Y[:, 0, :], copy).then_inc(q["y_act"], 1)

                act.wait_ge(s["table_ready"], l + 1)
                act.wait_ge(s["xg_cleared"], l + 1)
                last = act.value_load(table[0:1, T_LAST:T_LAST + 1], min_val=31, max_val=47)
                act.wait_ge(q["xg_turned"], 1)
                copy_rows(0)
                gate_up(0)
                act.wait_ge(q["xg_turned"], 2)
                act.wait_ge(q["up_done"], 1)
                copy_rows(1)
                copy_a(0)
                gate_up(1)
                act.wait_ge(q["xg_turned"], 3)
                act.wait_ge(q["up_done"], 2)
                copy_rows(2)
                copy_y(0)
                copy_a(1)
                with act.Fori(2, last + 1) as b:
                    gate_up(b)
                    act.wait_ge(q["xg_turned"], b + 2)
                    act.wait_ge(q["up_done"], b + 1)
                    copy_rows(b + 1)
                    act.wait_ge(q["scattered"], (b - 1) * 16)
                    copy_y(b - 1)
                    copy_a(b)
                act.wait_ge(q["scattered"], last * 16)
                copy_y(last)

            act.wait_ge(s["c_landed"], 16)
            act.activation(c_sig[:, :], c_col[:, :], ACT.Sigmoid).then_inc(s["sigmoid_ready"], 1)
            for k in range(KC):
                act.wait_ge(s["pool_mm"], k + 1)
                act.activation(pooled_t[:, k, :], ps[(k % 4) // 2][:, k % 2, :], copy).then_inc(s["pool_t_ready"], 1)
            norm(0)
            router(0)
            gates(0)
            experts(0)
            norm(1)
            for i in range(TILES):
                turned(V_KV + i, (s["kv_mm"], i - 1) if i >= 2 else None)
            for i in range(TILES):
                act.wait_ge(s["k_turn_mm"], i + 1)
                act.activation(k_t[:, :, i * P:(i + 1) * P],
                               ps[2][:, i % 2, 256:512].rearrange("p (h t) -> p h t", h=KVH), copy
                               ).then_inc(s["k_t_ready"], 1)
            for i in range(TILES):
                turned(V_Q + i, (s["q_mm"], i - 1) if i >= 2 else (s["kv_mm"], TILES))
                act.wait_ge(s["q_turn_mm"], i + 1)
                for j in range(2):
                    ins = act.activation(
                        q_t[:, 2 * i + j, :, :],
                        ps[3][:, :, :].rearrange("p b (a t) -> p (b a) t", a=4)[:, :, j * CHUNK:(j + 1) * CHUNK],
                        copy)
                ins.then_inc(s["q_t_ready"], 1)
            for n in range(NCHUNK):
                act.wait_ge(s["negm_ready"], n + 1)
                keys = CHUNK if n == 0 else P
                if n >= 1:
                    act.wait_ge(s["p_turn_mm"], n)
                act.activation(tiny[:, 16:24], tiny[:, 24:32], ACT.Exp)
                for g in range(8):
                    ins = act.activation(prob[:, g, 0:keys], ps[2 + n % 2][:, g // 4, (g % 4) * P:(g % 4) * P + keys],
                                         ACT.Exp, scale=QK_SCALE, bias=tiny[:, 8 + g:9 + g],
                                         accum_out=tiny[:, 32 + g:33 + g])
                ins.then_inc(s["prob_raw"], 1)
                act.wait_ge(s["p_turn_mm"], n + 1)
                if n >= 1:
                    act.wait_ge(s["pv_mm"], n)
                act.activation(prob_t, ps[0][:, :, :].rearrange("p a b -> p (a b)"), copy).then_inc(s["p_t_ready"], 1)
                act.wait_ge(s["pv_mm"], n + 1)
                if n >= 2 and n % 2 == 0:
                    act.wait_ge(s["wo_mm"], n // 2)
                act.activation(o_t[:, :, (n % 2) * CHUNK:(n % 2 + 1) * CHUNK],
                               ps[1][:, 0, :].rearrange("p (a t) -> p a t", a=NH // 2), copy
                               ).then_inc(s["o_t_ready"], 1)
            norm(2)
            router(1)
            gates(1)
            experts(1)
            norm(3)

        @block.vector
        def _(dve):
            chain = [0]

            def step(ins):
                chain[0] += 1
                ins.then_inc(s["dve_chain"], 1)

            def settle():
                dve.wait_ge(s["dve_chain"], chain[0])

            def link(ins):
                step(ins)
                settle()

            def ada(key):
                g = ada_at[key]
                part, h = divmod(key[1], 2)
                dst = vec[:, vslot[(key[0], part)], h * HALF:(h + 1) * HALF]
                dve.wait_ge(s["ada_mm"], g + 1)
                one = 1.0 if part in (1, 4) else 0.0
                dve.scalar_tensor_tensor(out=dst, in0=ps[3][:, g % 2, :], scalar=one, in1=dst,
                                         op0=ALU.add, op1=ALU.add).then_inc(s["ada_ready"], 1)

            def stats(q, i):
                u = q * TILES + i
                for h in range(2):
                    step(dve.bn_stats(stat[:, u % 2, h, :], xres[:, i, h * HALF:(h + 1) * HALF]))
                settle()
                link(dve.bn_aggr(mv[:, u % 2, 0:2], stat[:, u % 2, :, :].rearrange("p a b -> p (a b)")))
                dve.tensor_scalar(mv[:, u % 2, 2:3], mv[:, u % 2, 1:2], EPS, None, ALU.add
                                  ).then_inc(s["var_ready"], 1)

            def scale(q, i):
                u = q * TILES + i
                a = mv[:, u % 2, :]
                dve.wait_ge(s["std_ready"], u + 1)
                link(dve.reciprocal(a[:, 4:5], a[:, 3:4]))
                link(dve.tensor_tensor(a[:, 6:7], a[:, 4:5], a[:, 4:5], ALU.mult))
                link(dve.tensor_tensor(a[:, 6:7], a[:, 6:7], a[:, 2:3], ALU.mult))
                link(dve.tensor_scalar(a[:, 6:7], a[:, 6:7], -0.5, 1.5, ALU.mult, ALU.add))
                link(dve.tensor_tensor(a[:, 4:5], a[:, 4:5], a[:, 6:7], ALU.mult))
                dve.scalar_tensor_tensor(out=a[:, 5:6], in0=a[:, 0:1], scalar=-1.0, in1=a[:, 4:5],
                                         op0=ALU.mult, op1=ALU.mult).then_inc(s["scale_ready"], 1)

            def affine(q, i):
                u = q * TILES + i
                dve.wait_ge(s["zn_ready"], u + 1)
                dve.wait_ge(s["lnp_landed"], 32 * (q + 1))
                link(dve.tensor_tensor(xres[:, i, :], xres[:, i, :], lnp[:, 0, :], ALU.mult))
                dve.tensor_tensor(xres[:, i, :], xres[:, i, :], lnp[:, 1, :], ALU.add).then_inc(s["x_ready"], 1)

            def features(v, i, sc, sh):
                q = {0: 0, 4: 1, 8: 1, 12: 2}[v - i]
                dve.wait_ge(s["x_ready"], q * TILES + i + 1)
                if v >= 2:
                    dve.wait_ge(s["turn_mm"], v - 1)
                if v in (2, 3, 4, 5):
                    dve.wait_ge(s["h_stored"], 16 * min(v - 1, TILES))
                if v in (14, 15):
                    dve.wait_ge(s["h_stored"], 16 * (TILES + v - 13))
                link(dve.tensor_tensor(h_tile[v % 2], xres[:, i, :], vec[:, sc, :], ALU.mult))
                dve.tensor_tensor(h_tile[v % 2], h_tile[v % 2], vec[:, sh, :], ALU.add).then_inc(s["h_ready"], 1)

            def norm(q, make_z, after):
                for t in range(TILES + 2):
                    if t < TILES:
                        make_z(t)
                        stats(q, t)
                    if 0 <= t - 1 < TILES:
                        scale(q, t - 1)
                    if 0 <= t - 2 < TILES:
                        affine(q, t - 2)
                        after(t - 2)

            def split_bup(l):
                dve.wait_ge(s["bup_landed"], 48 * (l + 1))
                n = 3 * NE
                link(dve.tensor_copy(bup3[:, :], bup_f))
                link(dve.tensor_tensor(bup_f, bup_f, bup3[:, :], ALU.subtract))
                step(dve.tensor_copy(bup3[NE:2 * NE, :], bup_f[NE:2 * NE, :]))
                link(dve.tensor_copy(bup3[2 * NE:n, :], bup_f[2 * NE:n, :]))
                link(dve.tensor_tensor(bup_f[2 * NE:n, :], bup_f[2 * NE:n, :], bup3[2 * NE:n, :], ALU.subtract))
                dve.tensor_copy(bup3[2 * NE:n, :], bup_f[2 * NE:n, :]).then_inc(s["bup_ready"], 1)

            def route(l):
                iota_e = cst[:, C_EXP:C_EXP + NE]
                if l == 0:
                    dve.wait_ge(s["misc_landed"], 48)
                for i in range(TILES):
                    dve.wait_ge(s["logits_mm"], TILES * l + i + 1)
                    link(dve.tensor_tensor(logits[:, i, :], ps[2 + i // 2][:, i % 2, 0:NE], br[:, l, :], ALU.add))
                    link(dve.max(top8[:, i, :], logits[:, i, :]))
                    step(dve.max_index(idx8[:, i, :], top8[:, i, :], logits[:, i, :]))
                settle()
                dve.tensor_scalar(gsum[:, 0:TILES], top8[:, :, 0:1].rearrange("p i o -> p (i o)"), -1.0, None,
                                  ALU.mult).then_inc(s["neg_ready"], 1)
                link(dve.tensor_copy(idxf[:, :, :], idx8[:, :, 0:TOP]))
                for i in range(TILES):
                    step(dve.tensor_tensor(pick[:, i, :, :], iota_e.unsqueeze(1).to_broadcast([P, TOP, NE]),
                                           idxf[:, i, :].unsqueeze(2).to_broadcast([P, TOP, NE]), ALU.is_equal))
                settle()
                mask, t0 = routed[:, 0], routed[:, 1]
                step(dve.tensor_tensor(mask, pick[:, :, 0, :], pick[:, :, 1, :], ALU.add))
                link(dve.tensor_tensor(t0, pick[:, :, 2, :], pick[:, :, 3, :], ALU.add))
                link(dve.tensor_tensor(mask, mask, t0, ALU.add))
                dve.tensor_copy(mask_bf[:, :, :], mask).then_inc(s["mask_ready"], 1)
                link(dve.scalar_tensor_tensor(out=t0, in0=pick[:, :, 2, :], scalar=2.0, in1=pick[:, :, 1, :],
                                              op0=ALU.mult, op1=ALU.add))
                link(dve.scalar_tensor_tensor(out=vals[:, :, :, 2], in0=pick[:, :, 3, :], scalar=3.0, in1=t0,
                                              op0=ALU.mult, op1=ALU.add))
                dve.wait_ge(s["rank_mm"], l + 1)
                totals = ps[3][:, 1, TILES * NE:(TILES + 1) * NE]
                link(dve.tensor_tensor(t0, ps[3][:, 1, 0:TILES * NE].rearrange("p (i e) -> p i e", i=TILES),
                                       mask, ALU.mult))
                step(dve.tensor_scalar(rank[:, :, :], t0, -1.0, None, ALU.add))
                count, ends, reached = (blocks[:, j, :] for j in range(3))
                link(dve.tensor_scalar(count, totals, float(P), 1.0, ALU.is_gt, ALU.add))
                for j in (2, 3):
                    link(dve.scalar_tensor_tensor(out=count, in0=totals, scalar=float(j * P), in1=count,
                                                  op0=ALU.is_gt, op1=ALU.add))
                link(dve.tensor_tensor_scan(ends, bf_ones[:, 0:NE], count, 0.0, ALU.mult, ALU.add))
                part = cst[:, C_PART:C_PART + 1]
                link(dve.tensor_scalar(reached, ends, part, None, ALU.is_le))
                step(dve.tensor_reduce(blk_col[:, 0:1], reached, AX, ALU.add))
                link(dve.tensor_tensor(reached, reached, count, ALU.mult))
                link(dve.tensor_reduce(blk_col[:, 1:2], reached, AX, ALU.add))
                step(dve.tensor_scalar(blk_col[:, 0:1], blk_col[:, 0:1], float(NE - 1), None, ALU.min))
                link(dve.tensor_scalar(blk_col[:, 1:2], blk_col[:, 1:2], -1.0, part, ALU.mult, ALU.add))
                dve.tensor_scalar(blk_col[:, 1:2], blk_col[:, 1:2], float(TILES - 1), None, ALU.min
                                  ).then_inc(s["blkcol_ready"], 1)
                step(dve.tensor_copy(table[0:1, T_END:T_END + NE], ends[0:1, :]))
                step(dve.tensor_scalar(table[0:1, T_LAST:T_LAST + 1], ends[0:1, NE - 1:NE], -1.0, None, ALU.add))
                dve.wait_ge(s["blkrow_mm"], l + 1)
                settle()
                dve.tensor_copy(table[0:1, 0:2 * 64], ps[3][0:1, 0, 256:384]).then_inc(s["table_ready"], 1)
                dve.wait_ge(s["gexp_ready"], l + 1)
                link(dve.reciprocal(gsum[:, 2 * TILES:3 * TILES], gsum[:, TILES:2 * TILES]))
                link(dve.tensor_tensor(gate[:, :, :], gate[:, :, :],
                                       gsum[:, 2 * TILES:3 * TILES].unsqueeze(2).to_broadcast([P, TILES, TOP]),
                                       ALU.mult))
                for i in range(TILES):
                    step(dve.tensor_tensor(pick_g[:, i, :, :], pick[:, i, :, :],
                                           gate[:, i, :].unsqueeze(2).to_broadcast([P, TOP, NE]), ALU.mult))
                settle()
                step(dve.tensor_tensor(pick_col, pick_g[:, :, 0, :], pick_g[:, :, 1, :], ALU.add))
                link(dve.tensor_tensor(t0, pick_g[:, :, 2, :], pick_g[:, :, 3, :], ALU.add))
                dve.tensor_tensor(pick_col, pick_col, t0, ALU.add).then_inc(s["gcol_ready"], 1)

            def experts(l):
                q = m[l]
                T, Y, U, J = ps[0], ps[1], ps[2][:, 0, :], ps[3][:, 0, 0:4]

                def rows(b, ring_at):
                    dve.wait_ge(q["place_mm"], b + 1)
                    dve.tensor_reduce(row_f[:, :], J, AX, ALU.add).then_inc(q["sum_ready"], 1)
                    dve.wait_ge(q["sum_ready"], b + 1)
                    dve.tensor_scalar(row_i[:, :], row_f[:, :], float(NO_ROW), None, ALU.add).then_inc(q["rowf_ready"], 1)
                    dve.wait_ge(q["rowf_ready"], b + 1)
                    dve.tensor_copy(scatter_ring[:, ring_at], row_i[:, :]).then_inc(q["scatter_at_ready"], 1)

                def gather_rows(b):
                    dve.tensor_scalar(gather_at[:, :], row_i[:, :], 2, None, ALU.logical_shift_right
                                      ).then_inc(q["gather_at_ready"], 1)

                def copy_rows(b):
                    dve.tensor_copy(xT[:, 4:8, :].rearrange("p k t -> p (k t)"), T[:, 1, :]).then_inc(q["xT_dve"], 1)

                def clamp(b):
                    dve.wait_ge(q["up_done"], b + 1)
                    dve.tensor_scalar(glu, U[:, 0:UP:2], LIMIT, None, ALU.min).then_inc(q["glu_ready"], 1)
                    dve.tensor_scalar(lin, U[:, 1:UP:2], LIMIT, -LIMIT, ALU.min, ALU.max).then_inc(q["lin_ready"], 1)
                    dve.wait_ge(q["lin_ready"], b + 1)
                    dve.wait_ge(q["glu_ready"], b + 1)
                    dve.scalar_tensor_tensor(out=lin, in0=lin, scalar=1.0, in1=glu, op0=ALU.add, op1=ALU.mult
                                             ).then_inc(q["gl_ready"], 1)

                def finish_a(b):
                    dve.wait_ge(q["sig_ready"], b + 1)
                    dve.wait_ge(q["gl_ready"], b + 1)
                    dve.tensor_tensor(lin, lin, sig, ALU.mult).then_inc(q["a_ready"], 1)

                def copy_y(b):
                    dve.wait_ge(q["down_done"], b + 1)
                    dve.tensor_copy(y_sb[:, HALF:D], Y[:, 1, :]).then_inc(q["y_dve"], 1)

                last = dve.value_load(table[0:1, T_LAST:T_LAST + 1], min_val=31, max_val=47)
                dve.wait_ge(s["xg_cleared"], l + 1)
                rows(0, slice(0, 1))
                gather_rows(0)
                rows(1, slice(1, 2))
                dve.wait_ge(q["gathered"], 16)
                gather_rows(1)
                dve.wait_ge(q["xg_turned"], 1)
                copy_rows(0)
                for b in (0, 1):
                    clamp(b)
                    rows(b + 2, slice(b + 2, b + 3))
                    dve.wait_ge(q["gathered"], 16 * (b + 2))
                    gather_rows(b + 2)
                    dve.wait_ge(q["xg_turned"], b + 2)
                    copy_rows(b + 1)
                    finish_a(b)
                    if b:
                        copy_y(0)
                with dve.Fori(2, last + 1) as b:
                    clamp(b)
                    dve.wait_ge(q["scatter_taken"], b - 1)
                    rows(b + 2, bass.ds((b + 2) % 4, 1))
                    dve.wait_ge(q["gathered"], b * 16 + 32)
                    gather_rows(b + 2)
                    dve.wait_ge(q["xg_turned"], b + 2)
                    copy_rows(b + 1)
                    finish_a(b)
                    dve.wait_ge(q["scattered"], (b - 1) * 16)
                    copy_y(b - 1)
                dve.wait_ge(q["scattered"], last * 16)
                copy_y(last)

            def combine(l, i):
                y = y_in[i % 2]
                dve.wait_ge(s["y_landed_a" if i % 2 == 0 else "y_landed_b"], 16 * (2 * l + i // 2 + 1))
                dve.wait_ge(s["bdown_mm"], TILES * l + i + 1)
                dve.scalar_tensor_tensor(out=y[:, 0, :], in0=y[:, 0, :], scalar=gate[:, i, 0:1],
                                         in1=ps[i % 2][:, :, :].rearrange("p a b -> p (a b)"),
                                         op0=ALU.mult, op1=ALU.add).then_inc(s["dve_chain"], 1)
                chain[0] += 1
                settle()
                for k in range(1, TOP):
                    link(dve.scalar_tensor_tensor(out=y[:, 0, :], in0=y[:, k, :], scalar=gate[:, i, k:k + 1],
                                                  in1=y[:, 0, :], op0=ALU.mult, op1=ALU.add))
                link(dve.tensor_tensor(y[:, 0, :], y[:, 0, :], vec[:, 5, :], ALU.mult))
                dve.scalar_tensor_tensor(out=xres[:, i, :], in0=xres[:, i, :], scalar=ALPHA, in1=y[:, 0, :],
                                         op0=ALU.mult, op1=ALU.add).then_inc(s["combined"], 1)
                dve.wait_ge(s["combined"], TILES * l + i + 1)

            def add_mixed(q, i, psum, temp, done):
                dve.wait_ge(*done)
                link(dve.tensor_tensor(temp, psum[:, :, :].rearrange("p a b -> p (a b)"), vec[:, 2, :], ALU.mult))
                dve.scalar_tensor_tensor(out=xres[:, i, :], in0=xres[:, i, :], scalar=ALPHA, in1=temp,
                                         op0=ALU.mult, op1=ALU.add).then_inc(s["z_ready"], 1)
                dve.wait_ge(s["z_ready"], q // 2 * TILES + i + 1)

            def rope(out1, out2, x1, x2, cos, sin, ta, tb):
                step(dve.tensor_tensor(ta, x1, cos, ALU.mult))
                link(dve.tensor_tensor(tb, x2, sin, ALU.mult))
                link(dve.tensor_tensor(out1, ta, tb, ALU.subtract))
                step(dve.tensor_tensor(ta, x2, cos, ALU.mult))
                link(dve.tensor_tensor(tb, x1, sin, ALU.mult))
                return dve.tensor_tensor(out2, ta, tb, ALU.add)

            dve.wait_ge(s["c_landed"], 16)
            dve.wait_ge(s["sigmoid_ready"], 1)
            dve.tensor_tensor(c_sig[:, :], c_sig[:, :], c_col[:, :], ALU.mult).then_inc(s["c_act_ready"], 1)
            dve.memset(bf_ones[:, :], 1.0).then_inc(s["consts_cast"], 1)
            dve.wait_ge(s["const_landed"], 16)
            dve.tensor_copy(bf_sel[:, :], cst[0:3 * NE, C_SEL:C_SEL + NE]).then_inc(s["consts_cast"], 1)
            for i in range(TILES):
                step(dve.tensor_copy(vals[:, i, :, :], cst[:, C_VAL + 4 * i:C_VAL + 4 * i + 4].unsqueeze(1)
                                     .to_broadcast([P, NE, 4])))
            settle()
            dve.wait_ge(s["before_landed"], 16)
            dve.tensor_copy(bf_tri[:, :], work[:, 0, 0:P]).then_inc(s["consts_cast"], 1)
            dve.wait_ge(s["consts_cast"], 3)
            split_bup(0)

            dve.wait_ge(s["vecs_landed"], 96)
            for c in range(4):
                ada((0, c))
            dve.wait_ge(s["x_landed"], 16)
            dve.wait_ge(s["ada_ready"], 4)
            for i in range(TILES):
                link(dve.tensor_tensor(h_pool[:, i, :], xres[:, i, :], vec[:, 1, :], ALU.mult))
                dve.tensor_tensor(h_pool[:, i, :], h_pool[:, i, :], vec[:, 0, :], ALU.add).then_inc(s["hpool_ready"], 1)
            for c in range(4, 6):
                ada((0, c))
            dve.wait_ge(s["pscale_landed"], 16)
            dve.wait_ge(s["ada_ready"], 6)
            dve.tensor_tensor(vec[:, 2, :], vec[:, 2, :], work[:, 1, :], ALU.mult).then_inc(s["gate_scaled"], 1)
            dve.wait_ge(s["gate_scaled"], 1)
            for i in range(TILES):
                add_mixed(0, i, ps[i % 2], work[:, 2, :], (s["poolmix_mm"], i + 1))
            for c in range(6, 12):
                ada((0, c))
            dve.wait_ge(s["ada_ready"], 12)
            norm(0, lambda i: None, lambda i: features(V_ROUTE[0] + i, i, 4, 3))
            route(0)
            experts(0)

            def after_moe0(i):
                combine(0, i)
                if i == 1:
                    dve.wait_ge(s["vecs_landed"], 96 + 80)
                    for c in range(4):
                        ada(("kv", c))

            norm(1, after_moe0, lambda i: None)
            for c in range(6):
                ada((1, c))
            dve.wait_ge(s["ada_ready"], 22)
            for i in range(TILES):
                features(V_KV + i, i, 1, 0)
                dve.wait_ge(s["kv_mm"], i + 1)
                dve.tensor_copy(v_at[:, i, :], ps[2][:, i % 2, P:KV]).then_inc(s["v_ready"], 1)
                half = HD // 2
                cos = cst[:, C_COS + i * half:C_COS + (i + 1) * half].unsqueeze(1).to_broadcast([P, KVH, half])
                sin = cst[:, C_SIN + i * half:C_SIN + (i + 1) * half].unsqueeze(1).to_broadcast([P, KVH, half])
                kk = ps[2][:, i % 2, 0:P].rearrange("p (h s d) -> p h s d", h=KVH, s=2)
                dst = k_dup[:, i, :, :].rearrange("p h (c s d) -> p h c s d", c=2, s=2)
                ta, tb = (t[:, 0:KVH * half].rearrange("p (h d) -> p h d", h=KVH) for t in (rope_a, rope_b))
                link(rope(dst[:, :, 0, 0, :], dst[:, :, 0, 1, :], kk[:, :, 0, :], kk[:, :, 1, :], cos, sin, ta, tb))
                dve.tensor_copy(k_dup[:, i, :, HD:2 * HD], k_dup[:, i, :, 0:HD]).then_inc(s["k_rope_ready"], 1)
            dve.wait_ge(s["vecs_landed"], 96 + 80 + 48)
            for c in range(6, 12):
                ada((1, c))
            dve.wait_ge(s["ada_ready"], 28)
            for i in range(TILES):
                features(V_Q + i, i, 4, 3)
                dve.wait_ge(s["q_mm"], i + 1)
                if i:
                    dve.wait_ge(s["q_turn_mm"], i)
                half = HD // 2
                cos = cst[:, C_COS + i * half:C_COS + (i + 1) * half].unsqueeze(1).to_broadcast([P, NH, half])
                sin = cst[:, C_SIN + i * half:C_SIN + (i + 1) * half].unsqueeze(1).to_broadcast([P, NH, half])
                qq = ps[2][:, :, :].rearrange("p a (h s d) -> p (a h) s d", s=2, d=half)
                dst = q_rope.rearrange("p (h s d) -> p h s d", h=NH, s=2)
                ta, tb = (t.rearrange("p (h d) -> p h d", h=NH) for t in (rope_a, rope_b))
                rope(dst[:, :, 0, :], dst[:, :, 1, :], qq[:, :, 0, :], qq[:, :, 1, :], cos, sin, ta, tb
                     ).then_inc(s["q_rope_ready"], 1)
            split_bup(1)
            for n in range(NCHUNK):
                keys = CHUNK if n == 0 else P
                rows = ps[2 + n % 2][:, :, :].rearrange("p a (g k) -> p (a g) k", g=4)
                dve.wait_ge(s["score_mm"], n + 1)
                if n == 0:
                    step(dve.memset(prob[:, :, CHUNK:P], 0.0))
                link(dve.tensor_reduce(tiny[:, 0:8], rows[:, :, 0:keys], AX, ALU.max))
                link(dve.scalar_tensor_tensor(out=tiny[:, 0:8], in0=tiny[:, 0:8], scalar=QK_SCALE, in1=sink[:, :],
                                              op0=ALU.mult, op1=ALU.max))
                step(dve.tensor_tensor(tiny[:, 24:32], sink[:, :], tiny[:, 0:8], ALU.subtract))
                link(dve.tensor_scalar(tiny[:, 8:16], tiny[:, 0:8], -1.0, None, ALU.mult))
                dve.engine_nop().then_inc(s["negm_ready"], 1)
                dve.wait_ge(s["prob_raw"], n + 1)
                link(dve.tensor_tensor(tiny[:, 40:48], tiny[:, 32:40], tiny[:, 16:24], ALU.add))
                link(dve.reciprocal(tiny[:, 48:56], tiny[:, 40:48]))
                dve.tensor_tensor(prob[:, :, :], prob[:, :, :], tiny[:, 48:56].unsqueeze(2).to_broadcast([P, 8, P]),
                                  ALU.mult).then_inc(s["prob_ready"], 1)
                if n >= 1 and n % 2 == 0:
                    i = n // 2 - 1
                    add_mixed(2, i, ps[0], q_rope, (s["wo_mm"], i + 1))
            add_mixed(2, TILES - 1, ps[0], q_rope, (s["wo_mm"], TILES))
            norm(2, lambda i: None, lambda i: features(V_ROUTE[1] + i, i, 1, 0))
            route(1)
            experts(1)
            norm(3, lambda i: combine(1, i), lambda i: None)


INPUTS = ["x", "c", "w_ada", "b_ada", "ln_g", "ln_b", "pool_w", "pool_scale", "w_kv_ada", "b_kv_ada", "w_kv",
          "w_q", "w_o", "sink_rows", "w_router", "b_router", "w_up", "b_up", "w_down", "b_down",
          "const", "before", "pool_mats"]


def kernel(**inputs):
    import concourse.bacc as bacc
    from concourse.bass_utils import run_bass_kernel_spmd

    given = {k: np.asarray(v) for k, v in inputs.items()}
    heads = np.zeros((P, 8), np.int64)
    for kh in range(KVH):
        for par in range(2):
            for half in range(2):
                for r in range(2):
                    heads[r * CHUNK:(r + 1) * CHUNK, (par * 2 + kh) * 2 + half] = kh * 8 + half * 4 + r * 2 + par
    given["sink_rows"] = given["sinks"][0][heads]
    given["b_kv_ada"] = given["b_kv_ada"].reshape(1, -1)
    given["const"], given["before"], pool = constants()
    given["pool_mats"] = pool.reshape(P, -1)

    nc = bacc.Bacc("TRN2", target_bir_lowering=False, num_devices=1)
    arrays, args = {}, []
    for name in INPUTS:
        a = np.ascontiguousarray(given[name])
        arrays[f"in_{name}"] = a
        args.append(nc.dram_tensor(f"in_{name}", a.shape, mybir.dt.from_np(a.dtype), kind="ExternalInput").ap())
    args.append(nc.dram_tensor("out_0", (1, SEQ, D), F32, kind="ExternalOutput").ap())
    build(nc, *args)
    result = run_bass_kernel_spmd(nc, [arrays], core_ids=[0])
    return result.results[0]["out_0"]
```

```python
from contextlib import ExitStack

import concourse.bass as bass
import numpy as np
from concourse import mybir

F32 = mybir.dt.float32
BF16 = mybir.dt.bfloat16
I32 = mybir.dt.int32
U32 = mybir.dt.uint32
ALU = mybir.AluOpType
ACT = mybir.ActivationFunctionType
AX = mybir.AxisListType.X

P = 128
D = 1024
SEQ = 512
TILES = SEQ // P
KC = D // P
NE = 32
TOP = 4
FF = 256
KF = FF // P
UP = 2 * FF
HD = 64
NH = 16
KVH = 2
KV = 2 * KVH * HD
CHUNK = 64
NCHUNK = SEQ // CHUNK
WINDOWS = (2, 4, 8, 16)
PG = D // len(WINDOWS)
REACH = P + max(WINDOWS)
LIMIT = 7.0
SIG_ALPHA = 1.702
EPS = 1e-5
ALPHA = 4.0 ** 0.25
QK_SCALE = HD ** -0.5
HALF = 512
RING = 4
SLOT = KC * UP + KF * D
VEC = 6

C_IDENT = 0
C_SLOT = C_IDENT + P
C_BLOCK = C_SLOT + P
C_COS = C_BLOCK + TILES + 1
C_SIN = C_COS + TILES * HD // 2
C_EXP = C_SIN + TILES * HD // 2
C_PART = C_EXP + NE
C_VAL = C_PART + 1
C_SEL = C_VAL + 4 * TILES
C_ONE = C_SEL + NE
C_ALL = C_ONE + 1
PEELED = 4
PIECE = 256
KV_PIECES = 2 * D // PIECE
PIECES = 5 * D // PIECE
NO_ROW = TOP * SEQ
T_EXPERT, T_PLACE, T_END, T_LAST, T_PAIR, T_ALL = 0, 64, 128, 160, 161, 162


def constants():
    p = np.arange(P)
    c = np.zeros((P, C_ALL), np.float32)
    c[:, C_IDENT:C_IDENT + P] = np.eye(P)
    c[:, C_SLOT:C_SLOT + P] = np.arange(P)
    c[:, C_BLOCK:C_BLOCK + TILES + 1] = P * np.arange(TILES + 1)
    pos = np.arange(SEQ, dtype=np.float32)
    inv = (np.float32(10000.0) ** (-np.arange(0, HD, 2, dtype=np.float32) / HD)).astype(np.float32)
    ang = (pos[:, None] * inv[None, :]).astype(np.float32)
    for at, f in ((C_COS, np.cos), (C_SIN, np.sin)):
        c[:, at:at + TILES * HD // 2] = f(ang).reshape(TILES, P, HD // 2).transpose(1, 0, 2).reshape(P, -1)
    c[:, C_EXP:C_EXP + NE] = np.arange(NE)
    c[:, C_PART] = p
    for i in range(TILES):
        c[:, C_VAL + 4 * i] = TOP * p
        c[:, C_VAL + 4 * i + 1] = TOP * P * i
        c[:, C_VAL + 4 * i + 3] = -NO_ROW
    c[:, C_ONE] = 1.0
    c[:, C_SEL:C_SEL + NE] = (p[:, None] % NE) == np.arange(NE)
    before = (p[:, None] <= p[None, :]).astype(np.float32)
    pool = np.zeros((P, len(WINDOWS), 2, REACH), np.float32)
    t = np.arange(REACH)
    for g, w in enumerate(WINDOWS):
        inside = (t[None, :] >= p[:, None]) & (t[None, :] < p[:, None] + w)
        for first in (0, 1):
            count = np.minimum(t + 1, w) if first else np.full(REACH, w)
            pool[:, g, first] = np.where(inside, 1.0 / count.astype(np.float32), 0.0) - (t[None, :] == p[:, None])
    return c, before, pool


def stream_plan():
    plan, n = {}, 3
    for c in range(12):
        if c == 6:
            plan[("pool", 0, 0)] = n
            n += 1
        plan[("ada", 0, c)] = n
        n += 1
    start = [n]
    n += NE
    plan[("w_kv", 0, 0)] = n
    for h in range(2):
        plan[("w_q", 0, h)] = n + 1 + h
    plan[("w_o", 0, 0)] = n + 3
    for c in range(2):
        plan[("ada", 1, 6 + c)] = n + RING * (1 + c)
    plan[("w_o", 0, 1)] = n + RING * 3
    for c in range(4):
        plan[("ada", 1, 8 + c)] = n + RING + 1 + c % 2 + RING * (c // 2)
    n += RING * 4
    start.append(n)
    return plan, start


def build(nc, x, c, w_ada, b_ada, ln_g, ln_b, pool_w, pool_scale, w_kv_ada, b_kv_ada, w_kv,
          w_q, w_o, sink_rows, w_router, b_router, w_up, b_up, w_down, b_down,
          const, before, pool_mats, out):
    plan, expert_start = stream_plan()
    at_place = {n: k for k, n in plan.items()}
    for l in range(2):
        for e in range(NE):
            at_place[expert_start[l] + e] = ("expert", l, e)

    def uses(n):
        return sum(m in at_place for m in range(n % RING, n + 1, RING))

    def occupant(n):
        m = n - RING
        while m >= 0 and m not in at_place:
            m -= RING
        return at_place.get(m)

    ctx = ExitStack()
    with ctx:
        def sb(name, shape, dt=F32):
            return ctx.enter_context(nc.sbuf_tensor(name, shape, dt))

        def sem(name):
            return ctx.enter_context(nc.semaphore(name))

        h_dram = [nc.dram_tensor(f"h_rows{l}", [SEQ, D], F32, kind="Internal").ap() for l in range(2)]
        y_dram = [nc.dram_tensor(f"y_rows{l}", [NO_ROW, D], F32, kind="Internal").ap() for l in range(2)]

        ring = sb("ring", [P, RING * SLOT])
        xres = sb("xres", [P, TILES, D])
        big1 = sb("big1", [P, TILES * D])
        big2 = sb("big2", [P, TILES * D])
        vec = sb("vec", [P, VEC, D])
        lnp = sb("lnp", [P, 2, D])
        work = sb("work", [P, 4, D])
        spare = sb("spare", [P, 1536])
        cst = sb("cst", [P, C_ALL])
        bf_tri = sb("bf_tri", [P, P], BF16)
        bf_ones = sb("bf_ones", [P, P], BF16)
        bf_sel = sb("bf_sel", [3 * NE, NE], BF16)
        bup3 = sb("bup3", [3 * NE, UP], BF16)
        rank = sb("rank", [P, TILES, NE])
        onehot = sb("onehot", [P, TILES, P], BF16)
        rank_now = sb("rank_now", [P, TILES])
        vals = sb("vals", [P, TILES, NE, 4], BF16)
        wr = sb("wr", [P, KC, NE])
        c_col = sb("c_col", [P, KC])
        c_sig = sb("c_sig", [P, KC])
        br = sb("br", [P, 2, NE])
        sink = sb("sink", [P, 8])
        stat = sb("stat", [P, 2, 2, 6])
        mv = sb("mv", [P, 2, 8])
        tiny = sb("tiny", [P, 64])
        top8 = sb("top8", [P, TILES, 8])
        gate = sb("gate", [P, TILES, TOP])
        gsum = sb("gsum", [P, 3 * TILES])
        blk_col = sb("blk_col", [P, 2])
        table = sb("table", [1, T_ALL], I32)
        row_f = sb("row_f", [P, 1])
        row_i = sb("row_i", [P, 1], I32)
        gather_at = sb("gather_at", [P, 2], I32)
        scatter_ring = sb("scatter_ring", [P, 8], I32)
        scatter_at = sb("scatter_at", [P, 2], I32)

        h_pool = big1[:, :].rearrange("p (i d) -> p i d", i=TILES)
        q_t = big1[:, :].rearrange("p (n a t) -> p n a t", n=NCHUNK, a=NH // 2)
        pooled_t = big2[:, :].rearrange("p (k t) -> p k t", k=KC)
        kv_room = ring[:, 4 * SLOT - 2048:4 * SLOT]
        rope_room = ring[:, 3 * SLOT - 2048:3 * SLOT]
        k_t = kv_room[:, 0:KVH * SEQ].rearrange("p (h t) -> p h t", h=KVH)
        v_at = kv_room[:, 1024:1536].rearrange("p (i d) -> p i d", i=TILES)
        v_off = kv_room[:, 1536:2048].rearrange("p (i d) -> p i d", i=TILES)
        q_rope = big2[:, 2048:3072]
        o_t = [big2[:, at:at + 1024].rearrange("p (a t) -> p a t", a=NH // 2) for at in (0, 3072)]
        y_in = [b[:, :].rearrange("p (k d) -> p k d", k=TOP) for b in (big1, big2)]
        def h_tile(v):
            if V_KV <= v < V_ROUTE[1]:
                return work[:, v % 2, :]
            return big1[:, v % TILES * D:(v % TILES + 1) * D]

        h_t = [work[:, 2 + b, :].rearrange("p (k t) -> p k t", k=KC) for b in range(2)]
        xg = [work[:, 0, :], big2[:, 0:D]]
        y_sb = [work[:, 1, :], big2[:, D:2 * D]]
        xT = [r.rearrange("p (k t) -> p k t", k=KC) for r in (work[:, 2, :], big2[:, 2 * D:3 * D])]
        aT = work[:, 3, 0:256].rearrange("p (k t) -> p k t", k=KF)
        glu = work[:, 3, 256:512]
        lin = work[:, 3, 512:768]
        sig = work[:, 3, 768:1024]
        prob = work[:, 2, :].rearrange("p (g k) -> p g k", g=8)
        prob_t = work[:, 3, :]
        piece_in = [big1[:, p * KC * PIECE:(p + 1) * KC * PIECE].rearrange("p (k n) -> p k n", k=KC) for p in range(2)]
        piece_sum = [[big2[:, 3 * D + (2 * p + j) * PIECE:3 * D + (2 * p + j + 1) * PIECE] for j in range(2)]
                     for p in range(2)]
        diag = ring[:, SLOT - TILES * (TOP - 1) * P:SLOT].rearrange("p (i k c) -> p i k c", i=TILES, k=TOP - 1)
        bd = spare[0:NE, 0:D]
        gate_t = spare[0:NE, D:D + SEQ]
        bup_f = spare[0:3 * NE, 0:UP]
        rope_a = spare[:, 0:512]
        rope_b = spare[:, 512:1024]
        k_dup = rope_room[:, 0:1024].rearrange("p (i h d) -> p i h d", i=TILES, h=KVH)
        pick = spare[:, 0:512].rearrange("p (i k e) -> p i k e", i=TILES, k=TOP)
        pick_g = spare[:, 512:1024].rearrange("p (i k e) -> p i k e", i=TILES, k=TOP)
        scratch = big2[:, D:2 * D]
        logits = scratch[:, 0:TILES * NE].rearrange("p (i e) -> p i e", i=TILES)
        mask_bf = scratch[:, 128:192].bitcast(BF16).rearrange("p (i e) -> p i e", i=TILES)
        idx8 = scratch[:, 192:224].bitcast(U32).rearrange("p (i k) -> p i k", i=TILES)
        idxf = scratch[:, 224:240].rearrange("p (i k) -> p i k", i=TILES)
        blocks = scratch[:, 256:352].rearrange("p (a e) -> p a e", a=3)
        pick_col = spare[:, 1024:1152].rearrange("p (i e) -> p i e", i=TILES)
        routed = scratch[:, 512:768].rearrange("p (a i e) -> p a i e", a=2, i=TILES)

        ps = [ctx.enter_context(nc.psum_tensor(f"ps{i}", [P, 2, HALF], F32)) for i in range(4)]

        ident = cst[:, C_IDENT:C_IDENT + P]

        names = """const_landed c_landed before_landed x_landed misc_landed wr_landed vecs_landed lnp_landed
            bup_landed bdown_landed pscale_landed sigmoid_ready c_act_ready consts_cast ada_mm ada_ready
            hpool_ready pool_mm pool_t_ready poolmix_mm gate_scaled var_ready std_ready scale_ready zn_ready
            x_ready h_ready h_stored turn_mm h_t_ready logits_mm dve_chain mask_ready rank_mm blkcol_ready
            blkrow_mm table_ready bup_ready neg_ready gexp_ready gates_ready gcol_ready gcol_mm gate_t_ready bdown_mm
            y_landed_a y_landed_b combined kv_mm k_rope_ready k_turn_mm k_t_ready v_ready voff_landed q_mm
            q_rope_ready q_turn_mm q_t_ready score_mm negm_ready prob_raw prob_ready p_turn_mm p_t_ready pv_mm
            o_t_ready wo_mm z_ready xg_cleared out_stored sp_waited vec_cleared chunk_used bcast_mm bcast_done diag_ready fused_ready prep_step affine_step rows_landed gates_landed last_ready last_landed""".split()
        s = {n: sem(n) for n in names}
        slot_landed = [sem(f"slot_landed{r}") for r in range(RING)]
        down_landed = [sem(f"down_landed{r}") for r in range(RING)]
        moe_names = """up_weights_landed weights_landed pool_waited rank_taken onehot_ready place_mm sum_ready rowf_ready gather_at_ready
            scatter_at_ready gathered_a gathered_b xg_turned xT_act xT_dve up_done glu_ready lin_ready sig_ready gl_ready a_ready
            a_turned aT_ready down_done y_act y_dve scatter_taken scattered_a scattered_b""".split()
        m = [{n: sem(f"{n}{l}") for n in moe_names} for l in range(2)]
        m[0].update({n: sem(n) for n in ("piece_a", "piece_b", "part_step", "piece_free", "piece_added")})
        m[0]["piece"] = (m[0]["piece_a"], m[0]["piece_b"])
        for q in m:
            q["gathered"] = (q["gathered_a"], q["gathered_b"])
            q["scattered"] = (q["scattered_a"], q["scattered_b"])


        def moved(b, p):
            return (b - p) * 8 + 16

        block = ctx.enter_context(nc.Block())

        def slot_view(n, cols):
            r = n % RING
            return ring[:, r * SLOT:r * SLOT + cols]

        def wait_slot(eng, key):
            n = plan[key]
            eng.wait_ge(slot_landed[n % RING], 16 * uses(n))

        vslot = {(0, 0): 0, (0, 1): 1, (0, 2): 2, (0, 3): 3, (0, 4): 4, (0, 5): 5,
                 ("kv", 0): 0, ("kv", 1): 1, (1, 0): 2, (1, 1): 3, (1, 2): 4,
                 (1, 3): 0, (1, 4): 1, (1, 5): 5}
        gate_slot = (2, None, 4)
        vec_flat = vec[:, :, :].rearrange("p v d -> p (v d)")
        on_pe = (0, 1, 2, 3, 4, 5, 8, 9, 10, 11)
        on_dve = (6, 7)
        halves = [(v, h) for v in (3, 0, 1, 2, 3, 4, 0, 1, 5) for h in range(2)]
        plus_one = [n in (4, 5, 8, 9, 14, 15) for n in range(len(halves))]
        H_FIRST, H_LAST, H_ALL = 2, 12, 18

        used_up = {("pool", 0, 0): (s["poolmix_mm"], TILES), ("w_kv", 0, 0): (s["kv_mm"], TILES)}
        for h in range(2):
            used_up[("w_q", 0, h)] = (s["q_mm"], TILES)
            used_up[("w_o", 0, h)] = (s["wo_mm"], 2 * TILES)
        for h in range(12):
            used_up[("ada", 0, h)] = (s["ada_mm"], on_pe.index(h) + 1) if h in on_pe else (s["chunk_used"], on_dve.index(h) + 1)
        for j in range(6):
            used_up[("ada", 1, 6 + j)] = (s["chunk_used"], 2 + j + 1)

        V_ROUTE, V_KV, V_Q = (0, 12), 4, 8
        FUSED = ((4, 3), (1, 0), (1, 0))
        FUSED_TILE = (V_ROUTE[0], V_KV, V_ROUTE[1])

        def turn_bank(v):
            return ps[3] if V_KV <= v < V_ROUTE[1] else ps[v % 2]

        @block.sync
        def _(sp):
            def wait_free(n):
                prior = occupant(n)
                if prior is None:
                    return
                if prior[0] == "expert":
                    end = sp.value_load(table[0:1, T_END + prior[2]:T_END + prior[2] + 1],
                                        min_val=1, max_val=48)
                    sp.wait_ge(m[prior[1]]["down_done"], end)
                else:
                    sp.wait_ge(*used_up[prior])

            def load_static(key):
                kind, l, q = key
                n = plan[key]
                wait_free(n)
                done = slot_landed[n % RING]
                if kind == "pool":
                    sp.dma_start(slot_view(n, KC * PG).rearrange("p (a n) -> p a n", a=KC),
                                 pool_w[0].rearrange("g (j p) n -> p (g j) n", p=P)).then_inc(done, 16)
                    r = n % RING
                    sp.dma_start(ring[:, r * SLOT + KC * PG:r * SLOT + KC * PG + 8 * REACH],
                                 pool_mats).then_inc(down_landed[r], 16)
                    return
                width = KV if kind == "w_kv" else HALF
                src = {"ada": w_ada[l], "w_q": w_q[0], "w_kv": w_kv, "w_o": w_o[0]}[kind]
                src = src[:, q * width:(q + 1) * width]
                src = src.rearrange("(k p) n -> p k n", p=P) if kind == "w_o" else \
                    src.rearrange("(p k) n -> p k n", k=KC)
                sp.dma_start(slot_view(n, KC * width).rearrange("p (k n) -> p k n", k=KC),
                             src).then_inc(done, 16)

            def load_expert(l, e, r):
                sp.dma_start(ring[:, r * SLOT:r * SLOT + KC * UP],
                             w_up[l, bass.ds(e, 1)].rearrange("e (p k) n -> p (e k n)", k=KC)
                             ).then_inc(slot_landed[r], 16)
                sp.dma_start(ring[:, r * SLOT + KC * UP:(r + 1) * SLOT],
                             w_down[l, bass.ds(e, 1)].rearrange("e (p k) n -> p (e k n)", k=KF)
                             ).then_inc(down_landed[r], 16)

            def load_vectors(keys, rows, done):
                for key in keys:
                    src = b_kv_ada[:, key[1] * D:(key[1] + 1) * D] if key[0] == "kv" else \
                        b_ada[key[0]:key[0] + 1, key[1] * D:(key[1] + 1) * D]
                    sp.dma_start(vec[0:rows, vslot[key], :], src.to_broadcast([rows, D])
                                 ).then_inc(done, 16)

            def load_norm(q):
                l, j = divmod(q, 2)
                sp.dma_start(lnp[:, 0, :], ln_g[l, j:j + 1].to_broadcast([P, D])).then_inc(s["lnp_landed"], 16)
                sp.dma_start(lnp[:, 1, :], ln_b[l, j:j + 1].to_broadcast([P, D])).then_inc(s["lnp_landed"], 16)

            def load_router(l):
                sp.dma_start(wr[:, :, :], w_router[l].rearrange("(p k) e -> p k e", k=KC)
                             ).then_inc(s["wr_landed"], 16)

            def load_bup(l):
                for j in range(3):
                    sp.dma_start(bup_f[j * NE:(j + 1) * NE, :], b_up[l]).then_inc(s["bup_landed"], 16)

            def store_h(l):
                for i in range(TILES):
                    v = V_ROUTE[l] + i
                    sp.wait_ge(s["h_ready"], v + 1)
                    sp.dma_start(h_dram[l][i * P:(i + 1) * P, :], h_tile(v)).then_inc(s["h_stored"], 16)

            def expert_loads(l, following, meanwhile):
                n0 = expert_start[l]
                base = [16 * (uses(n0 + r) - 1) for r in range(RING)]
                base_down = [16 * (int(r == plan[("pool", 0, 0)] % RING) + l * NE // RING) for r in range(RING)]

                def pass_on(r, turn):
                    sp.wait_ge(slot_landed[r], turn * 16 + (base[r] + 16))
                    sp.sem_inc(m[l]["up_weights_landed"], 1)
                    sp.wait_ge(down_landed[r], turn * 16 + (base_down[r] + 16))
                    sp.sem_inc(m[l]["weights_landed"], 1)

                pass_on(0, 0)
                meanwhile()
                sp.wait_ge(s["table_ready"], l + 1)
                with sp.Fori(0, NE // RING - 1) as turn:
                    for r in range(RING):
                        pass_on((r + 1) % RING, turn + (r + 1) // RING)
                        e = turn * RING + r
                        end = sp.value_load(table[0:1, bass.ds(e + T_END, 1)], min_val=1, max_val=48)
                        sp.wait_ge(m[l]["down_done"], end)
                        load_expert(l, e + RING, r)
                for r in range(RING):
                    if r < RING - 1:
                        pass_on(r + 1, NE // RING - 1)
                    if r < len(following):
                        load_static(following[r])

            def collect(l):
                for i in range(TILES):
                    if i >= 2:
                        sp.wait_ge(s["combined"], TILES * l + i - 1)
                    elif i == 0:
                        pair = sp.value_load(table[0:1, T_PAIR:T_PAIR + 1], min_val=15, max_val=23)
                        for p in range(2):
                            sp.wait_ge(m[l]["scattered"][p], pair * 16 + 16)
                            sp.sem_inc(s["sp_waited"], 1)
                            sp.wait_ge(m[l]["gathered"][p], pair * 16 + 32)
                            sp.sem_inc(s["sp_waited"], 1)
                    sp.dma_start(y_in[i % 2], y_dram[l][TOP * P * i:TOP * P * (i + 1), :].rearrange(
                        "(p k) d -> p k d", k=TOP)).then_inc(s["y_landed_a" if i % 2 == 0 else "y_landed_b"], 16)

            items = sorted(plan, key=plan.get)
            first = [k for k in items if plan[k] < expert_start[0]]
            mid = [k for k in items if plan[k] > expert_start[0]]

            sp.dma_start(c_col[:, :], c.rearrange("b (p k) -> p (b k)", k=KC)).then_inc(s["c_landed"], 16)
            for k in first[:2]:
                load_static(k)
            load_vectors([(0, 1), (0, 0)], P, s["vecs_landed"])
            load_static(first[2])
            sp.dma_start(xres[:, :, :], x.rearrange("b (i p) d -> p (b i) d", p=P)).then_inc(s["x_landed"], 16)
            load_static(first[3])
            load_vectors([(0, 2), (0, 4)], P, s["gates_landed"])
            for k in first[4:7]:
                load_static(k)
            sp.dma_start(cst[:, :], const).then_inc(s["const_landed"], 16)
            sp.wait_ge(s["vec_cleared"], 1)
            load_vectors([(0, 3)], 1, s["rows_landed"])
            sp.dma_start(work[:, 0, 0:P], before).then_inc(s["before_landed"], 16)
            sp.dma_start(work[:, 1, :], pool_scale.to_broadcast([P, D])).then_inc(s["pscale_landed"], 16)
            for l in range(2):
                sp.dma_start(br[:, l, :], b_router[l:l + 1].to_broadcast([P, NE])).then_inc(s["misc_landed"], 16)
            sp.dma_start(sink[:, :], sink_rows).then_inc(s["misc_landed"], 16)
            load_router(0)
            load_bup(0)
            load_norm(0)
            load_vectors([(0, 5)], P, s["last_landed"])
            for k in first[7:]:
                load_static(k)
            for e in range(2):
                if e == 1:
                    store_h(0)
                wait_free(expert_start[0] + e)
                load_expert(0, e, e)
            sp.wait_ge(s["gcol_ready"], 1)
            sp.dma_start(bd, b_down[0]).then_inc(s["bdown_landed"], 16)
            load_router(1)

            def during_first():
                sp.wait_ge(m[0]["gathered_a"], 16)
                for e in (2, 3):
                    wait_free(expert_start[0] + e)
                    load_expert(0, e, e)
                sp.wait_ge(s["vec_cleared"], 1 + 5)
                load_vectors([("kv", 0), ("kv", 1), (1, 0), (1, 1), (1, 2)], 1, s["rows_landed"])
                sp.wait_ge(s["x_ready"], TILES)
                load_norm(1)

            def during_second():
                sp.wait_ge(s["x_ready"], 3 * TILES)
                load_norm(3)

            expert_loads(0, mid[:RING - 1], during_first)
            collect(0)
            load_static(("w_o", 0, 0))
            sp.wait_ge(s["vec_cleared"], 1 + 5 + 3)
            load_vectors([(1, 3), (1, 4), (1, 5)], 1, s["rows_landed"])
            for i in range(TILES):
                sp.wait_ge(s["v_ready"], i + 1)
            for i in range(TILES - 1):
                sp.dma_start(v_off[0:CHUNK, i, :], v_at[CHUNK:P, i, :]).then_inc(s["voff_landed"], 16)
                sp.dma_start(v_off[CHUNK:P, i, :], v_at[0:CHUNK, i + 1, :]).then_inc(s["voff_landed"], 16)
            for j in range(2):
                load_static(("ada", 1, 6 + j))
            load_static(("w_o", 0, 1))
            sp.wait_ge(s["x_ready"], 2 * TILES)
            load_norm(2)
            sp.wait_ge(s["q_rope_ready"], TILES)
            load_bup(1)
            for j in range(4):
                load_static(("ada", 1, 8 + j))
            for e in (1, 2, 0, 3):
                wait_free(expert_start[1] + e)
                load_expert(1, e, e)
            store_h(1)
            sp.wait_ge(s["gcol_ready"], 2)
            sp.dma_start(bd, b_down[1]).then_inc(s["bdown_landed"], 16)
            expert_loads(1, [], during_second)
            collect(1)
            for i in range(TILES):
                sp.wait_ge(*((s["x_ready"], 3 * TILES + i + 1) if i < TILES - 1 else (s["last_ready"], 1)))
                sp.dma_start(out[0, i * P:(i + 1) * P, :], xres[:, i, :]).then_inc(s["out_stored"], 16)
            sp.wait_ge(s["out_stored"], 16 * TILES)

        @block.gpsimd
        def _(pool):
            def prepare(q):
                sc, sh = FUSED[q]
                temp = work[:, 3 if q == 1 else 1, :]
                pool.wait_ge(s["lnp_landed"], 32 * (q + 1))
                if q == 0:
                    pool.wait_ge(s["bcast_done"], H_FIRST)
                    pool.wait_ge(s["ada_ready"], 8)
                    pool.wait_ge(s["gate_scaled"], 1)
                elif q == 1:
                    pool.wait_ge(s["bcast_done"], H_LAST)
                else:
                    pool.wait_ge(s["bcast_done"], H_ALL)
                    pool.wait_ge(s["turn_mm"], V_Q + TILES)
                pool.tensor_tensor(temp, vec[:, sc, :], lnp[:, 1, :], ALU.mult).then_inc(s["prep_step"], 1)
                pool.wait_ge(s["prep_step"], 2 * q + 1)
                pool.tensor_tensor(vec[:, sh, :], vec[:, sh, :], temp, ALU.add).then_inc(s["prep_step"], 1)
                pool.wait_ge(s["prep_step"], 2 * q + 2)
                pool.tensor_tensor(vec[:, sc, :], vec[:, sc, :], lnp[:, 0, :], ALU.mult).then_inc(s["fused_ready"], 1)

            def affine(q):
                for i in range(TILES - (q == 3)):
                    if q < 3:
                        pool.wait_ge(s["h_ready"], FUSED_TILE[q] + i + 1)
                    else:
                        pool.wait_ge(s["zn_ready"], 3 * TILES + i + 1)
                        pool.wait_ge(s["lnp_landed"], 32 * 4)
                    pool.tensor_tensor(xres[:, i, :], xres[:, i, :], lnp[:, 0, :], ALU.mult).then_inc(s["affine_step"], 1)
                    pool.wait_ge(s["affine_step"], q * TILES + i + 1)
                    pool.tensor_tensor(xres[:, i, :], xres[:, i, :], lnp[:, 1, :], ALU.add).then_inc(s["x_ready"], 1)

            def clear_vectors(slots):
                for v in slots:
                    pool.memset(vec[:, v, :], 0.0).then_inc(s["vec_cleared"], 1)

            def clear_rows(l):
                if l == 0:
                    pool.wait_ge(s["consts_cast"], 3)
                    pool.wait_ge(s["z_ready"], TILES)
                else:
                    pool.wait_ge(s["turn_mm"], V_Q + TILES)
                    pool.wait_ge(s["wo_mm"], 2 * TILES - 2)
                for r in xg:
                    pool.memset(r, 0.0).then_inc(s["xg_cleared"], 1)
                pool.wait_ge(s["xg_cleared"], 2 * (l + 1))

            def experts(l):
                q = m[l]


                def pick_rows(b):
                    e = pool.value_load(table[0:1, bass.ds(b + T_EXPERT, 1)], min_val=0, max_val=NE - 1)
                    n = pool.value_load(table[0:1, bass.ds(b + T_PLACE, 1)], min_val=0, max_val=TILES)
                    pool.tensor_tensor(rank_now[:, :], rank[:, :, bass.ds(e, 1)].rearrange("p i o -> p (i o)"),
                                       cst[:, bass.ds(n + C_BLOCK, 1)].to_broadcast([P, TILES]), ALU.subtract
                                       ).then_inc(q["rank_taken"], 1)
                    pool.wait_ge(q["rank_taken"], b + 1)
                    pool.sem_inc(q["pool_waited"], 1)
                    for i in range(TILES):
                        ins = pool.tensor_scalar(onehot[:, i, :], cst[:, C_SLOT:C_SLOT + P], rank_now[:, i:i + 1], None, ALU.is_equal)
                    ins.then_inc(q["onehot_ready"], 1)

                def gather(b, p):
                    pool.wait_ge(q["gather_at_ready"], b + 1)
                    pool.sem_inc(q["pool_waited"], 1)
                    pool.indirect_dma_start(
                        out=xg[p], out_offset=None, in_=h_dram[l][:, :],
                        in_offset=bass.IndirectOffsetOnAxis(ap=gather_at[:, p:p + 1], axis=0),
                        bounds_check=SEQ - 1, oob_is_err=False).then_inc(q["gathered"][p], 16)

                def scatter(b, p, last_pair=None):
                    pool.wait_ge(q["y_act"], b + 1)
                    pool.wait_ge(q["y_dve"], b + 1)
                    if last_pair is not None:
                        pool.wait_ge(q["scattered"][p], last_pair * 16)
                    elif not isinstance(b, int) or b >= 2:
                        pool.wait_ge(q["scattered"][p], moved(b, p) - 16)
                    pool.sem_inc(q["pool_waited"], 1)
                    pool.tensor_copy(scatter_at[:, p:p + 1], scatter_ring[:, bass.ds(b % 8, 1)]
                                     ).then_inc(q["scatter_taken"], 1)
                    pool.wait_ge(q["scatter_taken"], b + 1)
                    pool.sem_inc(q["pool_waited"], 1)
                    pool.indirect_dma_start(
                        out=y_dram[l][:, :], out_offset=bass.IndirectOffsetOnAxis(ap=scatter_at[:, p:p + 1], axis=0),
                        in_=y_sb[p], in_offset=None,
                        bounds_check=NO_ROW - 1, oob_is_err=False).then_inc(q["scattered"][p], 16)

                def body(b, p):
                    pool.wait_ge(q["xg_turned"], b + 1)
                    gather(b + 2, p)
                    pool.wait_ge(q["place_mm"], b + 3)
                    pick_rows(b + 3)
                    if not isinstance(b, int) or b >= 1:
                        scatter(b - 1, 1 - p)

                pool.wait_ge(s["table_ready"], l + 1)
                pick_rows(0)
                pool.wait_ge(q["place_mm"], 1)
                pick_rows(1)
                pool.wait_ge(s["h_stored"], 16 * TILES * (l + 1))
                gather(0, 0)
                pool.wait_ge(q["place_mm"], 2)
                pick_rows(2)
                gather(1, 1)
                if l == 0:
                    clear_vectors(range(5))
                for b in range(PEELED):
                    body(b, b % 2)
                last = pool.value_load(table[0:1, T_LAST:T_LAST + 1], min_val=31, max_val=47)
                pair = pool.value_load(table[0:1, T_PAIR:T_PAIR + 1], min_val=15, max_val=23)
                with pool.Fori(PEELED, last + 1, 2) as b:
                    for p in range(2):
                        body(b + p, p)
                scatter(last, 1, last_pair=pair)

            clear_vectors((3,))
            clear_rows(0)
            prepare(0)
            affine(0)
            experts(0)
            prepare(1)
            affine(1)
            pool.wait_ge(s["combined"], TILES)
            clear_vectors((0, 1, 5))
            prepare(2)
            clear_rows(1)
            affine(2)
            experts(1)
            affine(3)

        @block.tensor
        def _(pe):
            def ada(key):
                g = on_pe.index(key[1])
                skey = ("ada", key[0], key[1])
                w = slot_view(plan[skey], KC * HALF)
                wait_slot(pe, skey)
                if g >= 2:
                    pe.wait_ge(s["ada_ready"], g - 1)

                for k in range(KC):
                    mm = pe.matmul(ps[3][:, g % 2, :], c_sig[:, k:k + 1].to_broadcast([P, P]),
                                   w[:, k * HALF:(k + 1) * HALF], start=(k == 0), stop=(k == KC - 1))
                    if k == KC - 1:
                        mm.then_inc(s["ada_mm"], 1)

            def turn(v):
                bank = turn_bank(v)
                pe.wait_ge(s["h_ready"], v + 1)
                if v == V_KV:
                    pe.wait_ge(s["bcast_done"], H_LAST)
                elif V_KV < v < V_ROUTE[1]:
                    pe.wait_ge(s["h_t_ready"], v)
                elif v == V_ROUTE[1] + 1:
                    pe.wait_ge(s["z_ready"], 3 * TILES)
                elif v in (2, 3, 14, 15):
                    pe.wait_ge(s["h_t_ready"], v - 1)
                for k in range(KC):
                    mm = pe.transpose(bank[:, k // 4, (k % 4) * P:(k % 4 + 1) * P],
                                      h_tile(v)[:, k:D:KC], ident)
                mm.then_inc(s["turn_mm"], 1)

            def router(l):
                if l == 0:
                    turn(V_ROUTE[0])
                for i in range(TILES):
                    v = V_ROUTE[l] + i
                    if i + 1 < TILES and (l == 0 or i > 0):
                        turn(v + 1)
                    pe.wait_ge(s["h_t_ready"], v + 1)
                    if i == 0:
                        pe.wait_ge(s["wr_landed"], 16 * (l + 1))
                        pe.wait_ge(s["ada_ready"], len(on_pe))
                        if l:
                            pe.wait_ge(s["prob_raw"], NCHUNK)
                            pe.wait_ge(s["bcast_done"], H_ALL)
                    for k in range(KC):
                        mm = pe.matmul(ps[2 + i // 2][:, i % 2, 0:NE], h_t[v % 2][:, k, :], wr[:, k, :],
                                       start=(k == 0), stop=(k == KC - 1))
                    mm.then_inc(s["logits_mm"], 1)
                    if l == 1 and i == 0:
                        turn(v + 1)

            def ranks(l):
                pe.wait_ge(s["mask_ready"], l + 1)
                pe.wait_ge(s["consts_cast"], 3)
                for i in range(TILES):
                    for j in range(i + 1):
                        mm = pe.matmul(ps[3][:, 1, i * NE:(i + 1) * NE], bf_tri[:, :] if j == i else bf_ones[:, :],
                                       mask_bf[:, j, :], start=(j == 0), stop=(j == i))
                for j in range(TILES):
                    mm = pe.matmul(ps[3][:, 1, TILES * NE:(TILES + 1) * NE], bf_ones[:, :], mask_bf[:, j, :],
                                   start=(j == 0), stop=(j == TILES - 1))
                mm.then_inc(s["rank_mm"], 1)
                pe.wait_ge(s["blkcol_ready"], l + 1)
                for j in range(2):
                    mm = pe.matmul(ps[3][0:1, 0, 256 + 64 * j:320 + 64 * j], blk_col[:, j:j + 1], ident[:, 0:64],
                                   start=True, stop=True)
                mm.then_inc(s["blkrow_mm"], 1)

            def turn_gates(l):
                pe.wait_ge(s["gcol_ready"], l + 1)
                for i in range(TILES):
                    mm = pe.transpose(ps[2][0:NE, 0, i * P:(i + 1) * P], pick_col[:, i, :], ident)
                mm.then_inc(s["gcol_mm"], 1)

            def experts(l):
                q = m[l]
                T, Y, U, A, J = ps[0], ps[1], ps[2][:, 0, :], ps[2][:, 1, 0:256], ps[3][:, 0, 0:4]
                pe.wait_ge(s["table_ready"], l + 1)
                pe.wait_ge(s["gate_t_ready"], l + 1)
                pe.wait_ge(s["bup_ready"], l + 1)

                def places(b):
                    e = pe.value_load(table[0:1, bass.ds(b + T_EXPERT, 1)], min_val=0, max_val=NE - 1)
                    pe.wait_ge(q["onehot_ready"], b + 1)
                    for i in range(TILES):
                        mm = pe.matmul(J, onehot[:, i, :], vals[:, i, bass.ds(e, 1), :].rearrange("p a v -> p (a v)"),
                                       start=(i == 0), stop=(i == TILES - 1))
                    mm.then_inc(q["place_mm"], 1)

                def turn_rows(b, p):
                    pe.wait_ge(q["gathered"][p], moved(b, p))
                    if not isinstance(b, int) or b >= 1:
                        pe.wait_ge(q["xT_act"], b)
                        pe.wait_ge(q["xT_dve"], b)
                    for k in range(KC):
                        mm = pe.transpose(T[:, k // 4, (k % 4) * P:(k % 4 + 1) * P], xg[p][:, k:D:KC], ident)
                    mm.then_inc(q["xg_turned"], 1)

                def up(b, p):
                    e = pe.value_load(table[0:1, bass.ds(b + T_EXPERT, 1)], min_val=0, max_val=NE - 1)
                    at = (e % RING) * SLOT
                    if not isinstance(b, int) or b >= 1:
                        pe.wait_ge(q["lin_ready"], b)
                    pe.matmul(U, bf_sel[:, bass.ds(e, 1)].to_broadcast([3 * NE, P]), bup3[:, :],
                              start=True, stop=False)
                    pe.wait_ge(q["weights_landed"], e + 1)
                    pe.wait_ge(q["xT_act"], b + 1)
                    pe.wait_ge(q["xT_dve"], b + 1)
                    for k in range(KC):
                        mm = pe.matmul(U, xT[p][:, k, :], ring[:, bass.ds(at + k * UP, UP)],
                                       start=False, stop=(k == KC - 1))
                    mm.then_inc(q["up_done"], 1)

                def down(b):
                    e = pe.value_load(table[0:1, bass.ds(b + T_EXPERT, 1)], min_val=0, max_val=NE - 1)
                    at = (e % RING) * SLOT + KC * UP
                    pe.wait_ge(q["aT_ready"], b + 1)
                    if not isinstance(b, int) or b >= 1:
                        pe.wait_ge(q["y_act"], b)
                        pe.wait_ge(q["y_dve"], b)
                    for h in range(2):
                        for k in range(KF):
                            mm = pe.matmul(Y[:, h, :], aT[:, k, :], ring[:, bass.ds(at + k * D + h * HALF, HALF)],
                                           start=(k == 0), stop=(k == KF - 1))
                    mm.then_inc(q["down_done"], 1)

                def turn_a(b):
                    pe.wait_ge(q["a_ready"], b + 1)
                    for k in range(KF):
                        mm = pe.transpose(A[:, k * P:(k + 1) * P], lin[:, k:FF:KF], ident)
                    mm.then_inc(q["a_turned"], 1)

                def body(b, p):
                    up(b, p)
                    pe.wait_ge(q["sum_ready"], b + 3)
                    places(b + 3)
                    turn_rows(b + 1, 1 - p)
                    if not isinstance(b, int) or b >= 1:
                        down(b - 1)
                    turn_a(b)

                for b in range(3):
                    if b:
                        pe.wait_ge(q["sum_ready"], b)
                    places(b)
                turn_rows(0, 0)
                for b in range(PEELED):
                    body(b, b % 2)
                last = pe.value_load(table[0:1, T_LAST:T_LAST + 1], min_val=31, max_val=47)
                with pe.Fori(PEELED, last + 1, 2) as b:
                    for p in range(2):
                        body(b + p, p)
                down(last)
                pe.wait_ge(q["y_act"], last + 1)
                pe.wait_ge(q["y_dve"], last + 1)

            def spread(n, bank, users):
                v, h = halves[n]
                pe.wait_ge(*users)
                pe.matmul(bank, cst[:, C_ONE:C_ONE + 1].to_broadcast([P, P]), vec[:, v, h * HALF:(h + 1) * HALF],
                          start=True, stop=True).then_inc(s["bcast_mm"], 1)

            def collect(l, i):
                y = y_in[i % 2]
                pe.wait_ge(s["bdown_landed"], 16 * (l + 1))
                if i >= 2:
                    pe.wait_ge(s["combined"], TILES * l + i - 1)
                for h in range(2):
                    pe.matmul(ps[i % 2][:, h, :], gate_t[:, i * P:(i + 1) * P], bd[:, h * HALF:(h + 1) * HALF],
                              start=True, stop=False)
                pe.wait_ge(s["diag_ready"], TILES * l + i + 1)
                pe.wait_ge(s["y_landed_a" if i % 2 == 0 else "y_landed_b"], 16 * (2 * l + i // 2 + 1))
                for h in range(2):
                    for k in range(TOP - 1):
                        mm = pe.matmul(ps[i % 2][:, h, :], diag[:, i, k, :], y[:, k, h * HALF:(h + 1) * HALF],
                                       start=False, stop=(k == TOP - 2))
                mm.then_inc(s["bdown_mm"], 1)

            pe.wait_ge(s["c_act_ready"], 1)
            for c in range(6):
                ada((0, c))
            pool_n = plan[("pool", 0, 0)] % RING
            pw = ring[:, pool_n * SLOT:pool_n * SLOT + KC * PG].rearrange("p (a n) -> p a n", a=KC)
            pmat = ring[:, pool_n * SLOT + KC * PG:pool_n * SLOT + KC * PG + 8 * REACH].rearrange(
                "p (g f t) -> p g f t", g=len(WINDOWS), f=2)
            wait_slot(pe, ("pool", 0, 0))
            pe.wait_ge(down_landed[pool_n], 16)
            pe.wait_ge(s["hpool_ready"], TILES)
            for k in range(KC):
                bank = ps[(k % 4) // 2][:, k % 2, :]
                if k >= 4:
                    pe.wait_ge(s["pool_t_ready"], k - 3)
                for i in range(TILES):
                    width = min(REACH, SEQ - i * P)
                    mm = pe.matmul(bank[:, i * P:i * P + width], h_pool[:, i, k * P:(k + 1) * P],
                                   pmat[:, k // 2, int(i == 0), 0:width],
                                   start=(i == 0), stop=(i == TILES - 1), skip_group_check=True)
                mm.then_inc(s["pool_mm"], 1)
            for i in range(TILES):
                if i == 0:
                    pe.wait_ge(s["pool_t_ready"], KC)
                if i >= 2:
                    pe.wait_ge(s["z_ready"], i - 1)
                for g in range(len(WINDOWS)):
                    for j in range(2):
                        mm = pe.matmul(ps[i % 2][:, g // 2, (g % 2) * PG:(g % 2 + 1) * PG],
                                       pooled_t[:, 2 * g + j, i * P:(i + 1) * P], pw[:, 2 * g + j, :],
                                       start=(j == 0), stop=(j == 1))
                mm.then_inc(s["poolmix_mm"], 1)
            for c in on_pe[6:8]:
                ada((0, c))
            for n in range(H_FIRST):
                pe.wait_ge(s["chunk_used"], n + 1)
                spread(n, ps[3][:, n % 2, :], (s["ada_ready"], 8))
            pe.wait_ge(s["bcast_done"], H_FIRST)
            for c in on_pe[8:]:
                ada((0, c))
            pe.wait_ge(s["z_ready"], TILES)
            router(0)
            ranks(0)
            turn_gates(0)
            experts(0)
            pe.wait_ge(m[0]["piece_added"], PIECES)
            for n in range(H_FIRST, H_LAST):
                spread(n, ps[3][:, n % 2, :], (s["bcast_done"], n - 1))
            w_kv_at = slot_view(plan[("w_kv", 0, 0)], KC * KV)

            def keys_values(i):
                v = V_KV + i
                turn(v)
                if i == 0:
                    wait_slot(pe, ("w_kv", 0, 0))
                pe.wait_ge(s["h_t_ready"], v + 1)
                if i >= 2:
                    pe.wait_ge(s["k_rope_ready"], i - 1)
                    pe.wait_ge(s["v_ready"], i - 1)
                for k in range(KC):
                    mm = pe.matmul(ps[2][:, i % 2, 0:KV], h_t[v % 2][:, k, :], w_kv_at[:, k * KV:(k + 1) * KV],
                                   start=(k == 0), stop=(k == KC - 1))
                mm.then_inc(s["kv_mm"], 1)

            for i in range(TILES + 2):
                if i < TILES:
                    collect(0, i)
                if i >= 2:
                    keys_values(i - 2)

            def keys_turn():
                pe.wait_ge(s["k_rope_ready"], TILES)
                for i in range(TILES):
                    if i >= 2:
                        pe.wait_ge(s["k_t_ready"], i - 1)
                    for h in range(KVH):
                        mm = pe.transpose(ps[2][:, i % 2, 256 + h * P:256 + (h + 1) * P], k_dup[:, i, h, :], ident)
                    mm.then_inc(s["k_turn_mm"], 1)

            def query_turn(i):
                pe.wait_ge(s["q_rope_ready"], i + 1)
                pe.wait_ge(*((s["q_t_ready"], i) if i else (s["k_t_ready"], TILES)))
                for a in range(NH // 2):
                    mm = pe.transpose(ps[2][:, a // 4, (a % 4) * P:(a % 4 + 1) * P],
                                      q_rope[:, a * P:(a + 1) * P], ident)
                mm.then_inc(s["q_turn_mm"], 1)

            turn(V_Q)
            pe.wait_ge(s["combined"], TILES)
            for i in range(TILES):
                v = V_Q + i
                pe.wait_ge(s["h_t_ready"], v + 1)
                if i >= 2:
                    pe.wait_ge(s["q_rope_ready"], i - 1)
                for h in range(2):
                    if i == 0:
                        wait_slot(pe, ("w_q", 0, h))
                    w = slot_view(plan[("w_q", 0, h)], KC * HALF)
                    for k in range(KC):
                        mm = pe.matmul(ps[i % 2][:, h, :], h_t[v % 2][:, k, :], w[:, k * HALF:(k + 1) * HALF],
                                       start=(k == 0), stop=(k == KC - 1))
                mm.then_inc(s["q_mm"], 1)
                if i + 1 < TILES:
                    turn(v + 1)
                if i == 0:
                    keys_turn()
                else:
                    query_turn(i - 1)
            query_turn(TILES - 1)

            def scores(n):
                if n >= 2:
                    pe.wait_ge(s["prob_raw"], n - 1)
                first_key = max(n - 1, 0) * CHUNK
                for par in range(2):
                    for kh in range(KVH):
                        for half in range(2):
                            g = (par * 2 + kh) * 2 + half
                            a = kh * 4 + half * 2
                            mm = pe.matmul(ps[2 + n % 2][:, g // 4, (g % 4) * P:(g % 4 + 1) * P],
                                           q_t[par * HD:(par + 1) * HD, n, a:a + 2, :].rearrange("p a t -> p (a t)"),
                                           k_t[par * HD:(par + 1) * HD, kh, first_key:first_key + P],
                                           start=True, stop=True)
                mm.then_inc(s["score_mm"], 1)

            def values(n):
                pe.wait_ge(s["prob_ready"], n + 1)
                if n >= 1:
                    pe.wait_ge(s["p_t_ready"], n)
                for g in range(8):
                    mm = pe.transpose(ps[0][:, g // 4, (g % 4) * P:(g % 4 + 1) * P], prob[:, g, :], ident)
                mm.then_inc(s["p_turn_mm"], 1)
                pe.wait_ge(s["p_t_ready"], n + 1)
                if n >= 1:
                    pe.wait_ge(s["o_t_ready"], n)
                if n == 2:
                    pe.wait_ge(s["voff_landed"], 16 * 2 * (TILES - 1))
                src = v_at[:, max(n - 1, 0) // 2, :] if n % 2 or n == 0 else v_off[:, n // 2 - 1, :]
                for kh in range(KVH):
                    for par in range(2):
                        at = (par * 2 + kh) * 2 * P
                        mm = pe.matmul(ps[1][par * HD:(par + 1) * HD, 0, kh * 256:(kh + 1) * 256],
                                       src[:, kh * HD:(kh + 1) * HD], prob_t[:, at:at + 256],
                                       start=True, stop=True)
                mm.then_inc(s["pv_mm"], 1)

            def project(i, h):
                if i == 0:
                    wait_slot(pe, ("w_o", 0, h))
                pe.wait_ge(s["o_t_ready"], 2 * i + 2)
                if 2 * i + h:
                    pe.wait_ge(s["z_ready"], TILES + 2 * i + h)
                w = slot_view(plan[("w_o", 0, h)], KC * HALF)
                for a in range(KC):
                    mm = pe.matmul(ps[1][:, 1, :], o_t[i % 2][:, a, 0:P], w[:, a * HALF:(a + 1) * HALF],
                                   start=(a == 0), stop=(a == KC - 1))
                mm.then_inc(s["wo_mm"], 1)

            pe.wait_ge(s["q_t_ready"], TILES)
            scores(0)
            for n in range(NCHUNK):
                if n + 1 < NCHUNK:
                    scores(n + 1)
                else:
                    pe.wait_ge(s["chunk_used"], 2 + 6)
                    pe.wait_ge(s["prob_raw"], NCHUNK - 1)
                    for c in range(H_LAST, H_ALL):
                        spread(c, ps[2][:, c % 2, :], (s["bcast_done"], c - 1))
                if n >= 2:
                    project(n // 2 - 1, n % 2)
                values(n)
            project(TILES - 1, 0)
            turn(V_ROUTE[1])
            project(TILES - 1, 1)
            router(1)
            ranks(1)
            turn_gates(1)
            experts(1)
            for i in range(TILES):
                collect(1, i)

        @block.scalar
        def _(act):
            copy = ACT.Copy

            def norm_std(q, i):
                u = q * TILES + i
                act.wait_ge(s["var_ready"], u + 1)
                act.activation(mv[:, u % 2, 3:4], mv[:, u % 2, 2:3], ACT.Sqrt).then_inc(s["std_ready"], 1)

            def norm_apply(q, i):
                u = q * TILES + i
                act.wait_ge(s["scale_ready"], u + 1)
                act.activation(xres[:, i, :], xres[:, i, :], ACT.Identity, scale=mv[:, u % 2, 4:5],
                               bias=mv[:, u % 2, 5:6]).then_inc(s["zn_ready"], 1)

            def turned(v, used):
                act.wait_ge(s["turn_mm"], v + 1)
                if used:
                    act.wait_ge(*used)
                act.activation(h_t[v % 2].rearrange("p k t -> p (k t)"),
                               turn_bank(v)[:, :, :].rearrange("p a b -> p (a b)"), copy).then_inc(s["h_t_ready"], 1)

            def router(l):
                for i in range(TILES):
                    used = (s["logits_mm"], TILES * l + i - 1) if i >= 2 else \
                        (s["pv_mm"], NCHUNK) if l else (s["consts_cast"], 3)
                    turned(V_ROUTE[l] + i, used)
                    if l and i == 1:
                        norm_std(2, TILES - 1)
                    if l and i == 2:
                        norm_apply(2, TILES - 1)

            def gates(l):
                act.wait_ge(s["neg_ready"], l + 1)
                for i in range(TILES):
                    ins = act.activation(gate[:, i, :], top8[:, i, 0:TOP], ACT.Exp, bias=gsum[:, i:i + 1],
                                         accum_out=gsum[:, TILES + i:TILES + i + 1])
                ins.then_inc(s["gexp_ready"], 1)
                act.wait_ge(s["gcol_mm"], l + 1)
                act.activation(gate_t, ps[2][0:NE, 0, :], copy).then_inc(s["gate_t_ready"], 1)

            def experts(l):
                q = m[l]
                T, Y, A = ps[0], ps[1], ps[2][:, 1, 0:256]

                def copy_rows(b, p):
                    act.wait_ge(q["xg_turned"], b + 1)
                    if not isinstance(b, int) or b >= 2:
                        act.wait_ge(q["up_done"], b - 1)
                    act.activation(xT[p][:, 0:4, :].rearrange("p k t -> p (k t)"), T[:, 0, :], copy
                                   ).then_inc(q["xT_act"], 1)

                def gate_up(b):
                    act.wait_ge(q["glu_ready"], b + 1)
                    act.activation(sig, glu, ACT.Sigmoid, scale=SIG_ALPHA).then_inc(q["sig_ready"], 1)

                def copy_a(b):
                    act.wait_ge(q["a_turned"], b + 1)
                    act.activation(aT.rearrange("p k t -> p (k t)"), A, copy).then_inc(q["aT_ready"], 1)

                def copy_y(b, p, last_pair=None):
                    act.wait_ge(q["down_done"], b + 1)
                    if last_pair is not None:
                        act.wait_ge(q["scattered"][p], last_pair * 16)
                    elif not isinstance(b, int) or b >= 2:
                        act.wait_ge(q["scattered"][p], moved(b, p) - 16)
                    act.activation(y_sb[p][:, 0:HALF], Y[:, 0, :], copy).then_inc(q["y_act"], 1)

                def body(b, p):
                    gate_up(b)
                    copy_rows(b + 1, 1 - p)
                    if not isinstance(b, int) or b >= 1:
                        copy_y(b - 1, 1 - p)
                    copy_a(b)

                def load_piece(j, p, source, at):
                    if not isinstance(j, int):
                        act.wait_ge(q["piece_free"], j - 1)
                    act.dma_start(piece_in[p], source.rearrange("(p k) n -> p k n", k=KC)[:, :, bass.ds(at, PIECE)]
                                  ).then_inc(q["piece"][p], 16)

                act.wait_ge(s["table_ready"], l + 1)
                copy_rows(0, 0)
                for b in range(PEELED):
                    body(b, b % 2)
                    if l == 0 and b >= 2:
                        load_piece(b - 2, b % 2, w_kv_ada, (b - 2) * PIECE)
                last = act.value_load(table[0:1, T_LAST:T_LAST + 1], min_val=31, max_val=47)
                pair = act.value_load(table[0:1, T_PAIR:T_PAIR + 1], min_val=15, max_val=23)
                start = PEELED
                if l == 0:
                    with act.Fori(PEELED // 2, (KV_PIECES + 2) // 2) as pairs:
                        b = pairs * 2
                        for p in range(2):
                            body(b + p, p)
                            load_piece(b + (p - 2), p, w_kv_ada, (b + (p - 2)) * PIECE)
                    with act.Fori((KV_PIECES + 2) // 2, (PIECES + 2) // 2) as pairs:
                        b = pairs * 2
                        for p in range(2):
                            body(b + p, p)
                            load_piece(b + (p - 2), p, w_ada[1], (b + (p - 2 - KV_PIECES)) * PIECE)
                    start = PIECES + 2
                with act.Fori(start, last + 1, 2) as b:
                    for p in range(2):
                        body(b + p, p)
                copy_y(last, 1, last_pair=pair)
                for i in range(TILES):
                    for k in range(TOP - 1):
                        ins = act.activation(diag[:, i, k, :], ident, copy, scale=gate[:, i, k:k + 1])
                    ins.then_inc(s["diag_ready"], 1)

            act.wait_ge(s["c_landed"], 16)
            act.activation(c_sig[:, :], c_col[:, :], ACT.Sigmoid).then_inc(s["sigmoid_ready"], 1)
            for k in range(KC):
                act.wait_ge(s["pool_mm"], k + 1)
                act.activation(pooled_t[:, k, :], ps[(k % 4) // 2][:, k % 2, :], copy).then_inc(s["pool_t_ready"], 1)
            for i in range(TILES):
                norm_std(0, i)
                norm_apply(0, i)
            router(0)
            gates(0)
            experts(0)
            for t in range(TILES + 2):
                if t >= 2:
                    i = t - 2
                    turned(V_KV + i, (s["kv_mm"], i - 1) if i >= 2 else None)
                if t < TILES:
                    norm_std(1, t)
                    norm_apply(1, t)
            def keys():
                for i in range(TILES):
                    act.wait_ge(s["k_turn_mm"], i + 1)
                    act.activation(k_t[:, :, i * P:(i + 1) * P],
                                   ps[2][:, i % 2, 256:512].rearrange("p (h t) -> p h t", h=KVH), copy
                                   ).then_inc(s["k_t_ready"], 1)

            def queries(i):
                act.wait_ge(s["q_turn_mm"], i + 1)
                for j in range(2):
                    ins = act.activation(
                        q_t[:, 2 * i + j, :, :],
                        ps[2][:, :, :].rearrange("p b (a t) -> p (b a) t", a=4)[:, :, j * CHUNK:(j + 1) * CHUNK],
                        copy)
                ins.then_inc(s["q_t_ready"], 1)

            turned(V_Q, (s["kv_mm"], TILES))
            for i in range(TILES):
                if i + 1 < TILES:
                    turned(V_Q + i + 1, (s["q_mm"], i) if i >= 1 else (s["kv_mm"], TILES))
                if i == 0:
                    keys()
                else:
                    queries(i - 1)
            queries(TILES - 1)
            for n in range(NCHUNK):
                act.wait_ge(s["negm_ready"], n + 1)
                keys = CHUNK if n == 0 else P
                if n >= 1:
                    act.wait_ge(s["p_turn_mm"], n)
                act.activation(tiny[:, 16:24], tiny[:, 24:32], ACT.Exp)
                for g in range(8):
                    ins = act.activation(prob[:, g, 0:keys], ps[2 + n % 2][:, g // 4, (g % 4) * P:(g % 4) * P + keys],
                                         ACT.Exp, scale=QK_SCALE, bias=tiny[:, 8 + g:9 + g],
                                         accum_out=tiny[:, 32 + g:33 + g])
                ins.then_inc(s["prob_raw"], 1)
                act.wait_ge(s["p_turn_mm"], n + 1)
                if n >= 1:
                    act.wait_ge(s["pv_mm"], n)
                act.activation(prob_t, ps[0][:, :, :].rearrange("p a b -> p (a b)"), copy).then_inc(s["p_t_ready"], 1)
                act.wait_ge(s["pv_mm"], n + 1)
                if n >= 4 and n % 2 == 0:
                    act.wait_ge(s["wo_mm"], n - 2)
                act.activation(o_t[n // 2 % 2][:, :, (n % 2) * CHUNK:(n % 2 + 1) * CHUNK],
                               ps[1][:, 0, :].rearrange("p (a t) -> p a t", a=NH // 2), copy
                               ).then_inc(s["o_t_ready"], 1)
                if n == 4:
                    norm_std(2, 0)
                    norm_apply(2, 0)
            for i in (1, 2):
                norm_std(2, i)
                norm_apply(2, i)
            router(1)
            gates(1)
            experts(1)
            for i in range(TILES):
                norm_std(3, i)
                norm_apply(3, i)

        @block.vector
        def _(dve):
            chain = [0]

            def step(ins):
                chain[0] += 1
                ins.then_inc(s["dve_chain"], 1)

            def settle():
                dve.wait_ge(s["dve_chain"], chain[0])

            def link(ins):
                step(ins)
                settle()

            def ada(key):
                g = on_pe.index(key[1])
                part, h = divmod(key[1], 2)
                dst = vec[:, vslot[(key[0], part)], h * HALF:(h + 1) * HALF]
                dve.wait_ge(s["ada_mm"], g + 1)
                one = 1.0 if part in (1, 4) else 0.0
                dve.scalar_tensor_tensor(out=dst, in0=ps[3][:, g % 2, :], scalar=one, in1=dst,
                                         op0=ALU.add, op1=ALU.add).then_inc(s["ada_ready"], 1)

            def stats(q, i):
                u = q * TILES + i
                for h in range(2):
                    step(dve.bn_stats(stat[:, u % 2, h, :], xres[:, i, h * HALF:(h + 1) * HALF]))
                settle()
                link(dve.bn_aggr(mv[:, u % 2, 0:2], stat[:, u % 2, :, :].rearrange("p a b -> p (a b)")))
                dve.tensor_scalar(mv[:, u % 2, 2:3], mv[:, u % 2, 1:2], EPS, None, ALU.add
                                  ).then_inc(s["var_ready"], 1)

            def scale(q, i):
                u = q * TILES + i
                a = mv[:, u % 2, :]
                dve.wait_ge(s["std_ready"], u + 1)
                link(dve.reciprocal(a[:, 4:5], a[:, 3:4]))
                link(dve.tensor_tensor(a[:, 6:7], a[:, 4:5], a[:, 4:5], ALU.mult))
                link(dve.tensor_tensor(a[:, 6:7], a[:, 6:7], a[:, 2:3], ALU.mult))
                link(dve.tensor_scalar(a[:, 6:7], a[:, 6:7], -0.5, 1.5, ALU.mult, ALU.add))
                link(dve.tensor_tensor(a[:, 4:5], a[:, 4:5], a[:, 6:7], ALU.mult))
                dve.scalar_tensor_tensor(out=a[:, 5:6], in0=a[:, 0:1], scalar=-1.0, in1=a[:, 4:5],
                                         op0=ALU.mult, op1=ALU.mult).then_inc(s["scale_ready"], 1)

            def affine(q, i):
                u = q * TILES + i
                dve.wait_ge(s["zn_ready"], u + 1)
                dve.wait_ge(s["lnp_landed"], 32 * (q + 1))
                link(dve.tensor_tensor(xres[:, i, :], xres[:, i, :], lnp[:, 0, :], ALU.mult))
                dve.tensor_tensor(xres[:, i, :], xres[:, i, :], lnp[:, 1, :], ALU.add).then_inc(s["last_ready"], 1)

            def features(v, i, sc, sh, ready):
                dve.wait_ge(*ready)
                if V_KV + 2 <= v < V_ROUTE[1]:
                    dve.wait_ge(s["turn_mm"], v - 1)
                link(dve.tensor_tensor(h_tile(v), xres[:, i, :], vec[:, sc, :], ALU.mult))
                dve.tensor_tensor(h_tile(v), h_tile(v), vec[:, sh, :], ALU.add).then_inc(s["h_ready"], 1)

            def fused(q, i):
                dve.wait_ge(s["fused_ready"], q + 1)
                features(FUSED_TILE[q] + i, i, *FUSED[q], (s["zn_ready"], q * TILES + i + 1))

            def norm(q, make_z, after, later=lambda i: None):
                for t in range(TILES + 2):
                    if t < TILES:
                        make_z(t)
                        stats(q, t)
                    if 0 <= t - 1 < TILES:
                        after(t - 1)
                    if t < TILES:
                        scale(q, t)
                    if 0 <= t - 2 < TILES:
                        later(t - 2)

            def split_bup(l):
                dve.wait_ge(s["bup_landed"], 48 * (l + 1))
                n = 3 * NE
                link(dve.tensor_copy(bup3[:, :], bup_f))
                link(dve.tensor_tensor(bup_f, bup_f, bup3[:, :], ALU.subtract))
                step(dve.tensor_copy(bup3[NE:2 * NE, :], bup_f[NE:2 * NE, :]))
                link(dve.tensor_copy(bup3[2 * NE:n, :], bup_f[2 * NE:n, :]))
                link(dve.tensor_tensor(bup_f[2 * NE:n, :], bup_f[2 * NE:n, :], bup3[2 * NE:n, :], ALU.subtract))
                dve.tensor_copy(bup3[2 * NE:n, :], bup_f[2 * NE:n, :]).then_inc(s["bup_ready"], 1)

            def route(l):
                iota_e = cst[:, C_EXP:C_EXP + NE]
                if l == 0:
                    dve.wait_ge(s["misc_landed"], 48)
                for i in range(TILES):
                    dve.wait_ge(s["logits_mm"], TILES * l + i + 1)
                    link(dve.tensor_tensor(logits[:, i, :], ps[2 + i // 2][:, i % 2, 0:NE], br[:, l, :], ALU.add))
                    link(dve.max(top8[:, i, :], logits[:, i, :]))
                    step(dve.max_index(idx8[:, i, :], top8[:, i, :], logits[:, i, :]))
                settle()
                dve.tensor_scalar(gsum[:, 0:TILES], top8[:, :, 0:1].rearrange("p i o -> p (i o)"), -1.0, None,
                                  ALU.mult).then_inc(s["neg_ready"], 1)
                link(dve.tensor_copy(idxf[:, :, :], idx8[:, :, 0:TOP]))
                for i in range(TILES):
                    step(dve.tensor_tensor(pick[:, i, :, :], iota_e.unsqueeze(1).to_broadcast([P, TOP, NE]),
                                           idxf[:, i, :].unsqueeze(2).to_broadcast([P, TOP, NE]), ALU.is_equal))
                settle()
                mask, t0 = routed[:, 0], routed[:, 1]
                step(dve.tensor_tensor(mask, pick[:, :, 0, :], pick[:, :, 1, :], ALU.add))
                link(dve.tensor_tensor(t0, pick[:, :, 2, :], pick[:, :, 3, :], ALU.add))
                link(dve.tensor_tensor(mask, mask, t0, ALU.add))
                dve.tensor_copy(mask_bf[:, :, :], mask).then_inc(s["mask_ready"], 1)
                link(dve.scalar_tensor_tensor(out=t0, in0=pick[:, :, 2, :], scalar=2.0, in1=pick[:, :, 1, :],
                                              op0=ALU.mult, op1=ALU.add))
                link(dve.scalar_tensor_tensor(out=vals[:, :, :, 2], in0=pick[:, :, 3, :], scalar=3.0, in1=t0,
                                              op0=ALU.mult, op1=ALU.add))
                dve.wait_ge(s["rank_mm"], l + 1)
                totals = ps[3][:, 1, TILES * NE:(TILES + 1) * NE]
                link(dve.tensor_tensor(t0, ps[3][:, 1, 0:TILES * NE].rearrange("p (i e) -> p i e", i=TILES),
                                       mask, ALU.mult))
                step(dve.tensor_scalar(rank[:, :, :], t0, -1.0, None, ALU.add))
                count, ends, reached = (blocks[:, j, :] for j in range(3))
                link(dve.tensor_scalar(count, totals, float(P), 1.0, ALU.is_gt, ALU.add))
                for j in (2, 3):
                    link(dve.scalar_tensor_tensor(out=count, in0=totals, scalar=float(j * P), in1=count,
                                                  op0=ALU.is_gt, op1=ALU.add))
                link(dve.tensor_tensor_scan(ends, bf_ones[:, 0:NE], count, 0.0, ALU.mult, ALU.add))
                part = cst[:, C_PART:C_PART + 1]
                link(dve.tensor_scalar(reached, ends, part, None, ALU.is_le))
                step(dve.tensor_reduce(blk_col[:, 0:1], reached, AX, ALU.add))
                link(dve.tensor_tensor(reached, reached, count, ALU.mult))
                link(dve.tensor_reduce(blk_col[:, 1:2], reached, AX, ALU.add))
                link(dve.tensor_scalar(reached[:, 0:1], blk_col[:, 0:1], float(NE), float(TILES), ALU.is_ge, ALU.mult))
                step(dve.tensor_scalar(blk_col[:, 0:1], blk_col[:, 0:1], float(NE - 1), None, ALU.min))
                link(dve.tensor_scalar(blk_col[:, 1:2], blk_col[:, 1:2], -1.0, part, ALU.mult, ALU.add))
                link(dve.tensor_tensor(blk_col[:, 1:2], blk_col[:, 1:2], reached[:, 0:1], ALU.add))
                dve.tensor_scalar(blk_col[:, 1:2], blk_col[:, 1:2], float(TILES), None, ALU.min
                                  ).then_inc(s["blkcol_ready"], 1)
                step(dve.tensor_copy(table[0:1, T_END:T_END + NE], ends[0:1, :]))
                last = table[0:1, T_LAST:T_LAST + 1]
                link(dve.tensor_scalar(last, ends[0:1, NE - 1:NE], -1.0, None, ALU.add))
                link(dve.tensor_scalar(last, last, 1, None, ALU.bitwise_or))
                link(dve.tensor_scalar(table[0:1, T_PAIR:T_PAIR + 1], last, 1, None, ALU.logical_shift_right))
                link(dve.tensor_scalar(table[0:1, T_END + NE - 1:T_END + NE], last, 1.0, None, ALU.add))
                dve.wait_ge(s["blkrow_mm"], l + 1)
                settle()
                dve.tensor_copy(table[0:1, 0:2 * 64], ps[3][0:1, 0, 256:384]).then_inc(s["table_ready"], 1)
                dve.wait_ge(s["gexp_ready"], l + 1)
                link(dve.reciprocal(gsum[:, 2 * TILES:3 * TILES], gsum[:, TILES:2 * TILES]))
                link(dve.tensor_tensor(gate[:, :, :], gate[:, :, :],
                                       gsum[:, 2 * TILES:3 * TILES].unsqueeze(2).to_broadcast([P, TILES, TOP]),
                                       ALU.mult))
                for i in range(TILES):
                    step(dve.tensor_tensor(pick_g[:, i, :, :], pick[:, i, :, :],
                                           gate[:, i, :].unsqueeze(2).to_broadcast([P, TOP, NE]), ALU.mult))
                settle()
                step(dve.tensor_tensor(pick_col, pick_g[:, :, 0, :], pick_g[:, :, 1, :], ALU.add))
                link(dve.tensor_tensor(t0, pick_g[:, :, 2, :], pick_g[:, :, 3, :], ALU.add))
                dve.tensor_tensor(pick_col, pick_col, t0, ALU.add).then_inc(s["gcol_ready"], 1)

            def experts(l):
                q = m[l]
                T, Y, U, J = ps[0], ps[1], ps[2][:, 0, :], ps[3][:, 0, 0:4]

                def rows(b, ring_at):
                    dve.wait_ge(q["place_mm"], b + 1)
                    dve.tensor_reduce(row_f[:, :], J, AX, ALU.add).then_inc(q["sum_ready"], 1)
                    dve.wait_ge(q["sum_ready"], b + 1)
                    dve.tensor_scalar(row_i[:, :], row_f[:, :], float(NO_ROW), None, ALU.add).then_inc(q["rowf_ready"], 1)
                    dve.wait_ge(q["rowf_ready"], b + 1)
                    dve.tensor_copy(scatter_ring[:, ring_at], row_i[:, :]).then_inc(q["scatter_at_ready"], 1)

                def gather_rows(b, p):
                    if not isinstance(b, int) or b >= 2:
                        dve.wait_ge(q["gathered"][p], moved(b, p) - 16)
                    dve.tensor_scalar(gather_at[:, p:p + 1], row_i[:, :], 2, None, ALU.logical_shift_right
                                      ).then_inc(q["gather_at_ready"], 1)

                def copy_rows(b, p):
                    dve.wait_ge(q["xg_turned"], b + 1)
                    if not isinstance(b, int) or b >= 2:
                        dve.wait_ge(q["up_done"], b - 1)
                    dve.tensor_copy(xT[p][:, 4:8, :].rearrange("p k t -> p (k t)"), T[:, 1, :]).then_inc(q["xT_dve"], 1)

                def clamp(b):
                    dve.wait_ge(q["up_done"], b + 1)
                    dve.tensor_scalar(glu, U[:, 0:UP:2], LIMIT, None, ALU.min).then_inc(q["glu_ready"], 1)
                    dve.tensor_scalar(lin, U[:, 1:UP:2], LIMIT, -LIMIT, ALU.min, ALU.max).then_inc(q["lin_ready"], 1)
                    dve.wait_ge(q["lin_ready"], b + 1)
                    dve.wait_ge(q["glu_ready"], b + 1)
                    dve.scalar_tensor_tensor(out=lin, in0=lin, scalar=1.0, in1=glu, op0=ALU.add, op1=ALU.mult
                                             ).then_inc(q["gl_ready"], 1)

                def finish_a(b):
                    dve.wait_ge(q["sig_ready"], b + 1)
                    dve.wait_ge(q["gl_ready"], b + 1)
                    dve.tensor_tensor(lin, lin, sig, ALU.mult).then_inc(q["a_ready"], 1)

                def copy_y(b, p, last_pair=None):
                    dve.wait_ge(q["down_done"], b + 1)
                    if last_pair is not None:
                        dve.wait_ge(q["scattered"][p], last_pair * 16)
                    elif not isinstance(b, int) or b >= 2:
                        dve.wait_ge(q["scattered"][p], moved(b, p) - 16)
                    dve.tensor_copy(y_sb[p][:, HALF:D], Y[:, 1, :]).then_inc(q["y_dve"], 1)

                def body(b, p):
                    clamp(b)
                    if not isinstance(b, int):
                        dve.wait_ge(q["scatter_taken"], b - 3)
                    rows(b + 3, slice(b + 3, b + 4) if isinstance(b, int) else bass.ds((b + 3) % 8, 1))
                    finish_a(b)
                    gather_rows(b + 3, 1 - p)
                    copy_rows(b + 1, 1 - p)
                    if not isinstance(b, int) or b >= 1:
                        copy_y(b - 1, 1 - p)

                def piece(j, p):
                    w, t = piece_in[p], piece_sum[p]
                    dve.wait_ge(q["piece"][p], moved(j, p))
                    for k in range(KC):
                        c_k = c_sig[:, k:k + 1]
                        if k < 2:
                            ins = dve.tensor_scalar(t[k], w[:, k, :], c_k, None, ALU.mult)
                        else:
                            dve.wait_ge(q["part_step"], j * KC + (k - 1))
                            ins = dve.scalar_tensor_tensor(out=t[k % 2], in0=w[:, k, :], scalar=c_k, in1=t[k % 2],
                                                           op0=ALU.mult, op1=ALU.add)
                        ins.then_inc(q["part_step"], 1)
                    dve.wait_ge(q["part_step"], j * KC + KC)
                    dve.tensor_tensor(t[0], t[0], t[1], ALU.add).then_inc(q["piece_free"], 1)
                    dve.wait_ge(q["piece_free"], j + 1)
                    at = vec_flat[:, bass.ds(j * PIECE, PIECE)]
                    dve.tensor_tensor(at, at, t[0], ALU.add).then_inc(q["piece_added"], 1)
                    dve.wait_ge(q["piece_added"], j + 1)

                dve.wait_ge(s["xg_cleared"], 2 * (l + 1))
                for b in range(3):
                    rows(b, slice(b, b + 1))
                    gather_rows(b, b % 2)
                copy_rows(0, 0)
                for b in range(PEELED):
                    body(b, b % 2)
                last = dve.value_load(table[0:1, T_LAST:T_LAST + 1], min_val=31, max_val=47)
                pair = dve.value_load(table[0:1, T_PAIR:T_PAIR + 1], min_val=15, max_val=23)
                start = PEELED
                if l == 0:
                    dve.wait_ge(s["rows_landed"], 16 * (1 + 5))
                    with dve.Fori(PEELED // 2, (PEELED + PIECES) // 2) as pairs:
                        b = pairs * 2
                        for p in range(2):
                            body(b + p, p)
                            piece(b + (p - PEELED), p)
                    start = PEELED + PIECES
                with dve.Fori(start, last + 1, 2) as b:
                    for p in range(2):
                        body(b + p, p)
                copy_y(last, 1, last_pair=pair)

            def combine(l, i):
                f = ps[i % 2][:, :, :].rearrange("p a b -> p (a b)")
                dve.wait_ge(s["bdown_mm"], TILES * l + i + 1)
                dve.wait_ge(s["y_landed_a" if i % 2 == 0 else "y_landed_b"], 16 * (2 * l + i // 2 + 1))
                link(dve.scalar_tensor_tensor(out=f, in0=y_in[i % 2][:, TOP - 1, :], scalar=gate[:, i, TOP - 1:TOP],
                                              in1=f, op0=ALU.mult, op1=ALU.add))
                link(dve.tensor_tensor(f, f, vec[:, 5, :], ALU.mult))
                dve.scalar_tensor_tensor(out=xres[:, i, :], in0=xres[:, i, :], scalar=ALPHA, in1=f,
                                         op0=ALU.mult, op1=ALU.add).then_inc(s["combined"], 1)
                dve.wait_ge(s["combined"], TILES * l + i + 1)

            def add_mixed(i, psum, temp, done):
                dve.wait_ge(*done)
                link(dve.tensor_tensor(temp, psum[:, :, :].rearrange("p a b -> p (a b)"), vec[:, 2, :], ALU.mult))
                dve.scalar_tensor_tensor(out=xres[:, i, :], in0=xres[:, i, :], scalar=ALPHA, in1=temp,
                                         op0=ALU.mult, op1=ALU.add).then_inc(s["z_ready"], 1)
                dve.wait_ge(s["z_ready"], i + 1)

            def chunk(key, n, rows):
                v, h = halves[n]
                acc = vec[:, v, h * HALF:(h + 1) * HALF]
                w = slot_view(plan[key], KC * HALF)
                dve.wait_ge(s["rows_landed"], 16 * rows)
                wait_slot(dve, key)
                for k in range(KC):
                    ins = dve.scalar_tensor_tensor(out=acc, in0=w[:, k * HALF:(k + 1) * HALF], scalar=c_sig[:, k:k + 1],
                                                   in1=acc, op0=ALU.mult, op1=ALU.add)
                    if k < KC - 1:
                        link(ins)
                ins.then_inc(s["chunk_used"], 1)

            def spread(n, bank):
                v, h = halves[n]
                one = 1.0 if plus_one[n] else 0.0
                dve.wait_ge(s["bcast_mm"], n + 1)
                dve.tensor_scalar(vec[:, v, h * HALF:(h + 1) * HALF], bank, one, None, ALU.add
                                  ).then_inc(s["bcast_done"], 1)

            def rope(out1, out2, x1, x2, cos, sin, ta, tb):
                step(dve.tensor_tensor(ta, x1, cos, ALU.mult))
                link(dve.tensor_tensor(tb, x2, sin, ALU.mult))
                link(dve.tensor_tensor(out1, ta, tb, ALU.subtract))
                step(dve.tensor_tensor(ta, x2, cos, ALU.mult))
                link(dve.tensor_tensor(tb, x1, sin, ALU.mult))
                return dve.tensor_tensor(out2, ta, tb, ALU.add)

            dve.wait_ge(s["c_landed"], 16)
            dve.wait_ge(s["sigmoid_ready"], 1)
            dve.tensor_tensor(c_sig[:, :], c_sig[:, :], c_col[:, :], ALU.mult).then_inc(s["c_act_ready"], 1)
            dve.memset(bf_ones[:, :], 1.0).then_inc(s["consts_cast"], 1)
            dve.wait_ge(s["vecs_landed"], 32)
            for c in range(4):
                ada((0, c))
            dve.wait_ge(s["x_landed"], 16)
            dve.wait_ge(s["ada_ready"], 4)
            for i in range(TILES):
                link(dve.tensor_tensor(h_pool[:, i, :], xres[:, i, :], vec[:, 1, :], ALU.mult))
                dve.tensor_tensor(h_pool[:, i, :], h_pool[:, i, :], vec[:, 0, :], ALU.add).then_inc(s["hpool_ready"], 1)
            dve.wait_ge(s["gates_landed"], 32)
            for c in range(4, 6):
                ada((0, c))
            dve.wait_ge(s["pscale_landed"], 16)
            dve.wait_ge(s["ada_ready"], 6)
            dve.tensor_tensor(vec[:, 2, :], vec[:, 2, :], work[:, 1, :], ALU.mult).then_inc(s["gate_scaled"], 1)
            dve.wait_ge(s["gate_scaled"], 1)
            dve.wait_ge(s["const_landed"], 16)
            dve.tensor_copy(bf_sel[:, :], cst[0:3 * NE, C_SEL:C_SEL + NE]).then_inc(s["consts_cast"], 1)
            for i in range(TILES):
                step(dve.tensor_copy(vals[:, i, :, :], cst[:, C_VAL + 4 * i:C_VAL + 4 * i + 4].unsqueeze(1)
                                     .to_broadcast([P, NE, 4])))
            settle()
            dve.wait_ge(s["before_landed"], 16)
            dve.tensor_copy(bf_tri[:, :], work[:, 0, 0:P]).then_inc(s["consts_cast"], 1)
            dve.wait_ge(s["consts_cast"], 3)
            split_bup(0)

            chunk(("ada", 0, 6), 0, 1)
            for i in range(TILES):
                add_mixed(i, ps[i % 2], work[:, 2, :], (s["poolmix_mm"], i + 1))
                stats(0, i)
                if i == 1:
                    chunk(("ada", 0, 7), 1, 1)
                scale(0, i)
            for c in on_pe[6:8]:
                ada((0, c))
            for n in range(H_FIRST):
                spread(n, ps[3][:, n % 2, :])
            for i in range(TILES):
                fused(0, i)
                if i < 2:
                    dve.wait_ge(s["last_landed"], 16)
                    ada((0, 10 + i))
            route(0)
            experts(0)
            for n in range(H_FIRST, H_LAST):
                spread(n, ps[3][:, n % 2, :])

            def keys_values(i):
                dve.wait_ge(s["kv_mm"], i + 1)
                dve.tensor_copy(v_at[:, i, :], ps[2][:, i % 2, P:KV]).then_inc(s["v_ready"], 1)
                half = HD // 2
                cos = cst[:, C_COS + i * half:C_COS + (i + 1) * half].unsqueeze(1).to_broadcast([P, KVH, half])
                sin = cst[:, C_SIN + i * half:C_SIN + (i + 1) * half].unsqueeze(1).to_broadcast([P, KVH, half])
                kk = ps[2][:, i % 2, 0:P].rearrange("p (h s d) -> p h s d", h=KVH, s=2)
                dst = k_dup[:, i, :, :].rearrange("p h (c s d) -> p h c s d", c=2, s=2)
                ta, tb = (rope_room[:, at:at + KVH * half].rearrange("p (h d) -> p h d", h=KVH)
                          for at in (1024, 1024 + KVH * half))
                link(rope(dst[:, :, 0, 0, :], dst[:, :, 0, 1, :], kk[:, :, 0, :], kk[:, :, 1, :], cos, sin, ta, tb))
                dve.tensor_copy(k_dup[:, i, :, HD:2 * HD], k_dup[:, i, :, 0:HD]).then_inc(s["k_rope_ready"], 1)
                if i >= 2:
                    query_features(i - 2)

            def query_features(i):
                features(V_Q + i, i, 3, 2, (s["x_ready"], TILES + i + 1))

            norm(1, lambda i: combine(0, i), lambda i: fused(1, i), keys_values)
            for i in range(TILES):
                dve.wait_ge(s["q_mm"], i + 1)
                if i:
                    dve.wait_ge(s["q_turn_mm"], i)
                half = HD // 2
                cos = cst[:, C_COS + i * half:C_COS + (i + 1) * half].unsqueeze(1).to_broadcast([P, NH, half])
                sin = cst[:, C_SIN + i * half:C_SIN + (i + 1) * half].unsqueeze(1).to_broadcast([P, NH, half])
                qq = ps[i % 2][:, :, :].rearrange("p a (h s d) -> p (a h) s d", s=2, d=half)
                dst = q_rope.rearrange("p (h s d) -> p h s d", h=NH, s=2)
                ta, tb = (t.rearrange("p (h d) -> p h d", h=NH) for t in (rope_a, rope_b))
                rope(dst[:, :, 0, :], dst[:, :, 1, :], qq[:, :, 0, :], qq[:, :, 1, :], cos, sin, ta, tb
                     ).then_inc(s["q_rope_ready"], 1)
                if i + 2 < TILES:
                    query_features(i + 2)
                    chunk(("ada", 1, 6 + i), H_LAST + i, 1 + 5 + 3)

            def add_projected(i, h):
                u = 2 * i + h
                cols = slice(h * HALF, (h + 1) * HALF)
                temp = q_rope[:, cols]
                dve.wait_ge(s["wo_mm"], u + 1)
                link(dve.tensor_tensor(temp, ps[1][:, 1, :], vec[:, gate_slot[2], cols], ALU.mult))
                dve.scalar_tensor_tensor(out=xres[:, i, cols], in0=xres[:, i, cols], scalar=ALPHA, in1=temp,
                                         op0=ALU.mult, op1=ALU.add).then_inc(s["z_ready"], 1)
                dve.wait_ge(s["z_ready"], TILES + u + 1)

            def shift(n):
                keys = CHUNK if n == 0 else P
                rows = ps[2 + n % 2][:, :, :].rearrange("p a (g k) -> p (a g) k", g=4)
                dve.wait_ge(s["score_mm"], n + 1)
                link(dve.tensor_reduce(tiny[:, 0:8], rows[:, :, 0:keys], AX, ALU.max))
                link(dve.scalar_tensor_tensor(out=tiny[:, 0:8], in0=tiny[:, 0:8], scalar=QK_SCALE, in1=sink[:, :],
                                              op0=ALU.mult, op1=ALU.max))
                step(dve.tensor_tensor(tiny[:, 24:32], sink[:, :], tiny[:, 0:8], ALU.subtract))
                link(dve.tensor_scalar(tiny[:, 8:16], tiny[:, 0:8], -1.0, None, ALU.mult))
                dve.engine_nop().then_inc(s["negm_ready"], 1)

            link(dve.memset(prob[:, :, CHUNK:P], 0.0))
            shift(0)
            for n in range(NCHUNK):
                if n == NCHUNK - 1:
                    for c in range(H_LAST, H_ALL):
                        spread(c, ps[2][:, c % 2, :])
                dve.wait_ge(s["prob_raw"], n + 1)
                link(dve.tensor_tensor(tiny[:, 40:48], tiny[:, 32:40], tiny[:, 16:24], ALU.add))
                link(dve.reciprocal(tiny[:, 48:56], tiny[:, 40:48]))
                dve.tensor_tensor(prob[:, :, :], prob[:, :, :], tiny[:, 48:56].unsqueeze(2).to_broadcast([P, 8, P]),
                                  ALU.mult).then_inc(s["prob_ready"], 1)
                if n + 1 < NCHUNK:
                    shift(n + 1)
                if n >= 2:
                    add_projected(n // 2 - 1, n % 2)
                if n < 4:
                    chunk(("ada", 1, 8 + n), H_LAST + 2 + n, 1 + 5 + 3)
                if n == 4:
                    split_bup(1)
                if n >= 3 and n % 2:
                    stats(2, n // 2 - 1)
                if n == 4:
                    scale(2, 0)
            for i in (1, 2):
                scale(2, i)
            add_projected(TILES - 1, 0)
            for i in range(TILES - 1):
                fused(2, i)
            add_projected(TILES - 1, 1)
            stats(2, TILES - 1)
            scale(2, TILES - 1)
            fused(2, TILES - 1)
            route(1)
            experts(1)
            norm(3, lambda i: combine(1, i), lambda i: affine(3, i) if i == TILES - 1 else None)


INPUTS = ["x", "c", "w_ada", "b_ada", "ln_g", "ln_b", "pool_w", "pool_scale", "w_kv_ada", "b_kv_ada", "w_kv",
          "w_q", "w_o", "sink_rows", "w_router", "b_router", "w_up", "b_up", "w_down", "b_down",
          "const", "before", "pool_mats"]


def kernel(**inputs):
    import concourse.bacc as bacc
    from concourse.bass_utils import run_bass_kernel_spmd

    given = {k: np.asarray(v) for k, v in inputs.items()}
    heads = np.zeros((P, 8), np.int64)
    for kh in range(KVH):
        for par in range(2):
            for half in range(2):
                for r in range(2):
                    heads[r * CHUNK:(r + 1) * CHUNK, (par * 2 + kh) * 2 + half] = kh * 8 + half * 4 + r * 2 + par
    given["sink_rows"] = given["sinks"][0][heads]
    given["b_kv_ada"] = given["b_kv_ada"].reshape(1, -1)
    given["const"], given["before"], pool = constants()
    given["pool_mats"] = pool.reshape(P, -1)

    nc = bacc.Bacc("TRN2", target_bir_lowering=False, num_devices=1)
    arrays, args = {}, []
    for name in INPUTS:
        a = np.ascontiguousarray(given[name])
        arrays[f"in_{name}"] = a
        args.append(nc.dram_tensor(f"in_{name}", a.shape, mybir.dt.from_np(a.dtype), kind="ExternalInput").ap())
    args.append(nc.dram_tensor("out_0", (1, SEQ, D), F32, kind="ExternalOutput").ap())
    build(nc, *args)
    result = run_bass_kernel_spmd(nc, [arrays], core_ids=[0])
    return result.results[0]["out_0"]
```
